# Optimizing a Trainium2 kernel written in Bass

```python
import math
import jax, jax.numpy as jnp
from jax import lax
import numpy as np

D_MODEL = 1024
BATCH = 1
SEQ = 512
DEPTH = 1

HEAD_DIM = 64
A_HEADS = 8
A_KV = 2
A_GROUP = A_HEADS // A_KV
A_WINDOW = 128
B_HEADS = 8
B_KV = 2
B_GROUP = B_HEADS // B_KV
CMP_LEN = 32
CMP_STRIDE = 16
CMP_HIDDEN = 256
SLC_LEN = 64
SLC_TOPK = 16
B_WINDOW = 512
Q_BLOCK = 128
REL_BUCKETS = 32
REL_MAX_EXACT = 16
REL_MAX_DIST = 128
PEER_HEADS = 8
PEER_KEYS = 128
PEER_EXPERTS = PEER_KEYS * PEER_KEYS
PEER_QDIM = 256
PEER_HALF = PEER_QDIM // 2
PEER_TOPK = 16
PEER_CHUNK = 128
PLE_DIM = 256
EPS = 1e-6

A_QW = A_HEADS * HEAD_DIM
A_KVW = A_KV * HEAD_DIM
B_QW = B_HEADS * HEAD_DIM
B_KVW = B_KV * HEAD_DIM
IN_SPLIT_SIZES = (A_QW, A_KVW, A_KVW, B_QW, B_KVW, B_KVW, B_KVW, B_KVW, B_KVW, B_KVW, 3 * B_HEADS, 2 * D_MODEL)
IN_COLS = sum(IN_SPLIT_SIZES)

kernel_name = "hybrid_swa_nsa_peer_block"

def rmsnorm(x, g):
    xf = x.astype(jnp.float32)
    y = xf * lax.rsqrt(jnp.mean(xf * xf, axis=-1, keepdims=True) + EPS)
    return (y * g.astype(jnp.float32)).astype(x.dtype)

def rel_bucket(dist):
    d = jnp.maximum(dist, 0)
    large = REL_MAX_EXACT + (jnp.log(jnp.maximum(d, 1).astype(jnp.float32) / REL_MAX_EXACT)
                             / math.log(REL_MAX_DIST / REL_MAX_EXACT)
                             * (REL_BUCKETS - REL_MAX_EXACT)).astype(jnp.int32)
    large = jnp.minimum(large, REL_BUCKETS - 1)
    return jnp.where(d < REL_MAX_EXACT, d, large)

def masked_softmax(s, mask, sink=None):
    s = jnp.where(mask, s, -jnp.inf)
    m = jnp.max(s, axis=-1, keepdims=True)
    if sink is not None:
        m = jnp.maximum(m, sink)
    m = jnp.where(jnp.isfinite(m), m, 0.0)
    e = jnp.where(mask, jnp.exp(s - m), 0.0)
    den = jnp.sum(e, axis=-1, keepdims=True)
    if sink is not None:
        den = den + jnp.exp(sink - m)
    return e / jnp.maximum(den, 1e-30)

def banded_attention(q, k, v, bias_tab, window, sink=None):
    B, S, G, R, Dh = q.shape
    nblk = S // Q_BLOCK
    nb = window // Q_BLOCK
    kw_len = (nb + 1) * Q_BLOCK
    pad = nb * Q_BLOCK

    def windows(t):
        tp = jnp.pad(t, ((0, 0), (pad, 0), (0, 0), (0, 0))).reshape(B, nblk + nb, Q_BLOCK, G, Dh)
        return jnp.concatenate([tp[:, o:o + nblk] for o in range(nb + 1)], axis=2)

    kb, vb = windows(k), windows(v)
    qb = q.reshape(B, nblk, Q_BLOCK, G, R, Dh)
    s = jnp.einsum('bnqgrd,bnkgd->bngrqk', qb, kb).astype(jnp.float32) * (Dh ** -0.5)
    qi = jnp.arange(Q_BLOCK)[:, None]
    ki = jnp.arange(kw_len)[None, :]
    rel = pad + qi - ki
    bias = bias_tab[rel_bucket(rel)].astype(jnp.float32)
    s = s + jnp.transpose(bias, (2, 3, 0, 1))
    kpos = (jnp.arange(nblk)[:, None, None] - nb) * Q_BLOCK + ki[None]
    mask = (rel >= 0) & (rel < window) & (kpos >= 0)
    p = masked_softmax(s, mask[None, :, None, None], sink)
    o = jnp.einsum('bngrqk,bnkgd->bnqgrd', p.astype(v.dtype), vb)
    return o.reshape(B, S, G, R, Dh)

def compress_blocks(t, pos, w1, w2):
    B, S, G, Dh = t.shape
    nch = S // CMP_STRIDE
    r = CMP_LEN // CMP_STRIDE
    n_cmp = nch - r + 1
    ch = t.reshape(B, nch, CMP_STRIDE, G, Dh)
    blocks = jnp.concatenate([ch[:, o:o + n_cmp] for o in range(r)], axis=2)
    blocks = blocks + pos[None, None, :, None, :]
    flat = jnp.transpose(blocks, (0, 1, 3, 2, 4)).reshape(B, n_cmp, G, CMP_LEN * Dh)
    return jax.nn.gelu(flat @ w1) @ w2

def nsa_attention(q, k_c, v_c, k_s, v_s, k_w, v_w, gates, cmp_pos, ck_w1, ck_w2, cv_w1, cv_w2, bias_tab):
    B, S, G, R, Dh = q.shape
    scale = Dh ** -0.5
    kc = compress_blocks(k_c, cmp_pos, ck_w1, ck_w2)
    vc = compress_blocks(v_c, cmp_pos, cv_w1, cv_w2)
    n_cmp = kc.shape[1]
    n_slc = S // SLC_LEN
    k_sel = min(SLC_TOPK, n_slc)
    ci = jnp.arange(n_cmp)[:, None] * CMP_STRIDE
    sj = jnp.arange(n_slc)[None, :] * SLC_LEN
    overlap = (jnp.clip(jnp.minimum(ci + CMP_LEN, sj + SLC_LEN) - jnp.maximum(ci, sj), 0)
               .astype(jnp.float32) / CMP_LEN)
    cend = jnp.arange(n_cmp) * CMP_STRIDE + CMP_LEN - 1
    ks_blocks = jnp.transpose(k_s.reshape(B, n_slc, SLC_LEN, G, Dh), (0, 3, 1, 2, 4))
    vs_blocks = jnp.transpose(v_s.reshape(B, n_slc, SLC_LEN, G, Dh), (0, 3, 1, 2, 4))
    tab_g = jnp.transpose(bias_tab, (1, 0, 2)).astype(jnp.float32)
    bi = jnp.arange(B)[:, None, None, None]
    gi = jnp.arange(G)[None, None, :, None]
    jidx = jnp.arange(n_slc)
    forced_score = float(R + 1)

    def block_fn(args):
        qc, tpos = args
        sc = jnp.einsum('bqgrd,bcgd->bqgrc', qc, kc).astype(jnp.float32) * scale
        cmask = cend[None, :] <= tpos[:, None]
        pc = masked_softmax(sc, cmask[None, :, None, None, :])
        o_cmp = jnp.einsum('bqgrc,bcgd->bqgrd', pc.astype(vc.dtype), vc)
        ps = jnp.einsum('bqgrc,cj->bqgj', pc, overlap)
        jt = (tpos // SLC_LEN)[:, None]
        forced = (jidx[None] == 0) | (jidx[None] == jt) | (jidx[None] == jt - 1)
        future = jidx[None] > jt
        ps = jnp.where(future[None, :, None, :], -1.0,
                       jnp.where(forced[None, :, None, :], forced_score, ps))
        _, idx = lax.top_k(ps, k_sel)
        kg = ks_blocks[bi, gi, idx].reshape(B, Q_BLOCK, G, k_sel * SLC_LEN, Dh)
        vg = vs_blocks[bi, gi, idx].reshape(B, Q_BLOCK, G, k_sel * SLC_LEN, Dh)
        kpos = (idx[..., None] * SLC_LEN + jnp.arange(SLC_LEN)).reshape(B, Q_BLOCK, G, k_sel * SLC_LEN)
        dist = tpos[None, :, None, None] - kpos
        ss = jnp.einsum('bqgrd,bqgkd->bqgrk', qc, kg).astype(jnp.float32) * scale
        bias = jnp.moveaxis(tab_g[gi, rel_bucket(dist)], -1, 3)
        psel = masked_softmax(ss + bias, (dist >= 0)[:, :, :, None, :])
        o_slc = jnp.einsum('bqgrk,bqgkd->bqgrd', psel.astype(vg.dtype), vg)
        return o_cmp, o_slc

    nblk = S // Q_BLOCK
    qcs = jnp.transpose(q.reshape(B, nblk, Q_BLOCK, G, R, Dh), (1, 0, 2, 3, 4, 5))
    tposs = jnp.arange(S).reshape(nblk, Q_BLOCK)
    o_cmp, o_slc = lax.map(block_fn, (qcs, tposs))
    o_cmp = jnp.transpose(o_cmp, (1, 0, 2, 3, 4, 5)).reshape(B, S, G, R, Dh)
    o_slc = jnp.transpose(o_slc, (1, 0, 2, 3, 4, 5)).reshape(B, S, G, R, Dh)
    o_win = banded_attention(q, k_w, v_w, bias_tab, B_WINDOW)
    g = jax.nn.sigmoid(gates.astype(jnp.float32)).reshape(B, S, 3, G, R, 1).astype(q.dtype)
    return g[:, :, 0] * o_cmp + g[:, :, 1] * o_slc + g[:, :, 2] * o_win

def peer(h, w_q, sub_k1, sub_k2, u, v):
    B, S, D = h.shape
    q = (h @ w_q).reshape(B, S, PEER_HEADS, 2, PEER_HALF)
    s1 = jnp.einsum('bshd,nd->bshn', q[..., 0, :], sub_k1).astype(jnp.float32)
    s2 = jnp.einsum('bshd,nd->bshn', q[..., 1, :], sub_k2).astype(jnp.float32)
    v1, i1 = lax.top_k(s1, PEER_TOPK)
    v2, i2 = lax.top_k(s2, PEER_TOPK)
    cand = (v1[..., :, None] + v2[..., None, :]).reshape(B, S, PEER_HEADS, PEER_TOPK * PEER_TOPK)
    cidx = (i1[..., :, None] * PEER_KEYS + i2[..., None, :]).reshape(B, S, PEER_HEADS, PEER_TOPK * PEER_TOPK)
    sc, pos = lax.top_k(cand, PEER_TOPK)
    eidx = jnp.take_along_axis(cidx, pos, axis=-1)
    gate = jax.nn.softmax(sc, axis=-1)
    T = B * S
    nchunk = T // PEER_CHUNK
    hc = h.reshape(nchunk, PEER_CHUNK, D)
    ec = eidx.reshape(nchunk, PEER_CHUNK, PEER_HEADS, PEER_TOPK)
    gc = gate.reshape(nchunk, PEER_CHUNK, PEER_HEADS, PEER_TOPK)

    def chunk_fn(args):
        hx, ex, gx = args
        act = jax.nn.gelu(jnp.einsum('td,thkd->thk', hx, u[ex]))
        return jnp.einsum('thk,thkd->td', (gx.astype(act.dtype) * act), v[ex])

    return lax.map(chunk_fn, (hc, ec, gc)).reshape(B, S, D)

def setup_inputs(seed: int = 0) -> dict:
    key = jax.random.key(seed)
    ks = jax.random.split(key, 32)
    f32 = jnp.float32

    def nrm(k, shape, scale):
        return jax.random.normal(k, shape, f32) * scale

    L, D = DEPTH, D_MODEL
    return {
        'x': nrm(ks[0], (BATCH, SEQ, D), 1.0),
        'p': nrm(ks[1], (DEPTH, BATCH, SEQ, PLE_DIM), 1.0),
        'g_mix': 1.0 + nrm(ks[2], (L, D), 0.05),
        'w_in': nrm(ks[3], (L, D, IN_COLS), D ** -0.5),
        'a_sink': nrm(ks[4], (L, A_KV, A_GROUP), 0.5),
        'rel_bias': nrm(ks[5], (REL_BUCKETS, A_HEADS + B_HEADS), 0.5),
        'cmp_pos': nrm(ks[6], (L, CMP_LEN, HEAD_DIM), 0.1),
        'cmp_k_w1': nrm(ks[7], (L, CMP_LEN * HEAD_DIM, CMP_HIDDEN), (CMP_LEN * HEAD_DIM) ** -0.5),
        'cmp_k_w2': nrm(ks[8], (L, CMP_HIDDEN, HEAD_DIM), CMP_HIDDEN ** -0.5),
        'cmp_v_w1': nrm(ks[9], (L, CMP_LEN * HEAD_DIM, CMP_HIDDEN), (CMP_LEN * HEAD_DIM) ** -0.5),
        'cmp_v_w2': nrm(ks[10], (L, CMP_HIDDEN, HEAD_DIM), CMP_HIDDEN ** -0.5),
        'w_up_a': nrm(ks[11], (L, A_QW, D), A_QW ** -0.5),
        'w_up_b': nrm(ks[12], (L, B_QW, D), B_QW ** -0.5),
        'w_o': nrm(ks[13], (L, D, D), D ** -0.5),
        'g_ffn': 1.0 + nrm(ks[14], (L, D), 0.05),
        'peer_wq': nrm(ks[15], (L, D, PEER_HEADS * PEER_QDIM), D ** -0.5),
        'peer_k1': nrm(ks[16], (L, PEER_KEYS, PEER_HALF), PEER_HALF ** -0.5),
        'peer_k2': nrm(ks[17], (L, PEER_KEYS, PEER_HALF), PEER_HALF ** -0.5),
        'peer_u': nrm(ks[18], (L, PEER_EXPERTS, D), D ** -0.5),
        'peer_v': nrm(ks[19], (L, PEER_EXPERTS, D), 0.5),
        'g_ple': 1.0 + nrm(ks[20], (L, D), 0.05),
        'w_ple_gate': nrm(ks[21], (L, D, D), D ** -0.5),
        'w_ple': nrm(ks[22], (L, PLE_DIM, D), PLE_DIM ** -0.5),
        'g_final': 1.0 + nrm(ks[23], (D,), 0.05),
    }

def reference(x, p, g_mix, w_in, a_sink, rel_bias, cmp_pos, cmp_k_w1, cmp_k_w2, cmp_v_w1, cmp_v_w2,
              w_up_a, w_up_b, w_o, g_ffn, peer_wq, peer_k1, peer_k2, peer_u, peer_v,
              g_ple, w_ple_gate, w_ple, g_final):
    B, S, D = x.shape
    bias_a = rel_bias[:, :A_HEADS].reshape(REL_BUCKETS, A_KV, A_GROUP)
    bias_b = rel_bias[:, A_HEADS:].reshape(REL_BUCKETS, B_KV, B_GROUP)
    split_at = np.cumsum(IN_SPLIT_SIZES)[:-1].tolist()
    for i in range(DEPTH):
        h = rmsnorm(x, g_mix[i])
        z = h @ w_in[i]
        (aq, ak, av, bq, bkc, bvc, bks, bvs, bkw, bvw, bgates, mgates) = jnp.split(z, split_at, axis=-1)
        sink = a_sink[i].astype(jnp.float32)[None, None, :, :, None, None]
        o_a = banded_attention(aq.reshape(B, S, A_KV, A_GROUP, HEAD_DIM),
                               ak.reshape(B, S, A_KV, HEAD_DIM), av.reshape(B, S, A_KV, HEAD_DIM),
                               bias_a, A_WINDOW, sink)
        y_a = o_a.reshape(B, S, A_QW) @ w_up_a[i]
        kv = lambda t: t.reshape(B, S, B_KV, HEAD_DIM)
        o_b = nsa_attention(bq.reshape(B, S, B_KV, B_GROUP, HEAD_DIM), kv(bkc), kv(bvc), kv(bks), kv(bvs),
                            kv(bkw), kv(bvw), bgates, cmp_pos[i], cmp_k_w1[i], cmp_k_w2[i],
                            cmp_v_w1[i], cmp_v_w2[i], bias_b)
        y_b = o_b.reshape(B, S, B_QW) @ w_up_b[i]
        mg = jax.nn.sigmoid(mgates.reshape(B, S, 2, D))
        x = x + (mg[:, :, 0] * y_a + mg[:, :, 1] * y_b) @ w_o[i]
        x = x + peer(rmsnorm(x, g_ffn[i]), peer_wq[i], peer_k1[i], peer_k2[i], peer_u[i], peer_v[i])
        x = x + jax.nn.sigmoid(rmsnorm(x, g_ple[i]) @ w_ple_gate[i]) * (p[i] @ w_ple[i])
    return rmsnorm(x, g_final)


_drawn_inputs = setup_inputs


def setup_inputs(seed=0):
    import zlib

    import numpy as np

    out = dict(_drawn_inputs(seed))
    spreads = {}
    factors = {'a_sink': 6.374, 'g_ple': 6.548}
    for name, (base, spread) in spreads.items():
        noise = np.random.default_rng([zlib.crc32(name.encode()), seed]).standard_normal(out[name].shape)
        drawn = base * np.exp(spread * noise) if base else spread * noise
        out[name] = __import__('jax').numpy.asarray(drawn.astype(out[name].dtype))
    for name, factor in factors.items():
        out[name] = (out[name] * factor).astype(out[name].dtype)
    return out
```

```python
import math
from contextlib import ExitStack

import numpy as np

import concourse.bass as bass
from concourse import mybir

D = 1024
S = 512
P = 128
TILES = S // P
KC = D // P
HALF = 512
DH = 64
HEADS = 8
GROUPS = 2
REP = HEADS // GROUPS
BUCKETS, MAX_EXACT, MAX_DIST = 32, 16, 128
CMP_LEN, CMP_STRIDE, CMP_HID = 32, 16, 256
NCMP = S // CMP_STRIDE - CMP_LEN // CMP_STRIDE + 1
LPAIR = CMP_LEN // 2
PK = 128
PH = 8
TK = 16
COLS = PH * TK
PLE = 256
EPS = 1e-6
NEG = -1e30
SCALE = DH ** -0.5

RUNS = [(0, 1, 16), (1, 1, 8), (2, 1, 5), (3, 1, 4), (4, 1, 3), (5, 3, 2), (8, 8, 1)]
NCAND = sum(na * nb for _, na, nb in RUNS)

ZT = 13
NAT_COLS = 3 * 128 + 24
NATB = 4
B_NAT = ZT
B_W1 = B_NAT + NATB
B_MG = B_W1 + 8
B_WO = B_MG + 3 * KC
B_WQ = B_WO + KC
NBLK = B_WQ + 2 * PH
RING = 6

SLOTS = 8
GRP = 4


def bucket_onehot():
    width = S + P
    out = np.zeros((BUCKETS + 1, width), np.float32)
    for y in range(width):
        dist = y - (P - 1)
        if dist < 0:
            out[BUCKETS, y] = 1.0
            continue
        b = dist
        if dist >= MAX_EXACT:
            b = MAX_EXACT + int(math.log(dist / MAX_EXACT) / math.log(MAX_DIST / MAX_EXACT) * (BUCKETS - MAX_EXACT))
            b = min(b, BUCKETS - 1)
        out[b, y] = 1.0
    return out


def build(nc, a, out):
    f32, i32, u32 = mybir.dt.float32, mybir.dt.int32, mybir.dt.uint32
    ALU, ACT, AX = mybir.AluOpType, mybir.ActivationFunctionType, mybir.AxisListType
    V, T, A, G = nc.vector, nc.tensor, nc.scalar, nc.gpsimd
    ctx = ExitStack()
    with ctx:
        def sb(name, shape, dt=f32):
            return ctx.enter_context(nc.sbuf_tensor(name, shape, dt))

        def sem(name):
            return ctx.enter_context(nc.semaphore(name))

        xs = sb("xs", [P, TILES, D])
        hn = sb("hn", [P, TILES, D])
        ring = sb("ring", [P, RING, D])
        ident = sb("ident", [P, P])
        zero = sb("zero", [P, P])
        small = sb("small", [P, 8 + 8 + CMP_LEN + 8 + 256 + 256])
        gmix, gple = small[:, 0:8], small[:, 8:16]
        posT = small[:, 16:48]
        sink = small[:, 48:56]
        w2 = small[:, 56:312].rearrange("p (v h d) -> p v h d", v=2, h=2)
        pkeys = small[:, 312:568].rearrange("p (h n) -> p h n", h=2)
        eidx = sb("eidx", [P, TILES * COLS + 1], i32)
        gate = sb("gate", [P, TILES * COLS])
        stat = sb("stat", [P, 64])
        ARENA = 33860
        ar = sb("arena", [P, ARENA])

        def place(start, shape, dt=None):
            n = int(np.prod(shape))
            assert start + n <= ARENA, (start, shape)
            v = ar[:, start:start + n]
            if dt is not None:
                v = v.bitcast(dt)
            if len(shape) == 2:
                v = v.rearrange("p (a b) -> p a b", a=shape[0])
            if len(shape) == 3:
                v = v.rearrange("p (a b c) -> p a b c", a=shape[0], b=shape[1])
            return v, start + n

        at = 0
        hT, at = place(at, [KC, S])
        at_q = at
        qk, at = place(at, [11, S])
        vn, at = place(at, [TILES, NAT_COLS])
        gsig, at = place(at, [TILES, 24])
        biasB, at = place(at, [HEADS, S])
        biasA, at = place(at, [HEADS, 2 * P])
        sw, at = place(at, [3, REP, S])
        pts, at = place(at, [4, S])
        cm, at = place(at, [2, LPAIR, GROUPS * NCMP])
        gT, at = place(at, [2, 2, GROUPS * NCMP])
        kcT, at = place(at, [NCMP])
        vcs, at = place(at, [GROUPS, DH])
        cmask, at = place(at, [TILES, NCMP])
        oTA, at = place(at, [4, S])
        oTB, at = place(at, [4, S])
        rbias, _ = place(at_q + 11 * S + TILES * NAT_COLS + TILES * 24 + 6 * S * 2, [S + P])
        mT, _ = place(at_q, [KC, S])
        sg, _ = place(at_q + 11 * S + TILES * NAT_COLS + TILES * 24, [2, 2, S])
        qT, ra = place(at_q, [2 * PH, S])
        s12, ra = place(ra, [2, 2 * PH, PK])
        rest, ra = place(ra, [2 * PH, PK])
        eqt, _ = place(0, [COLS, NCAND])
        vals, ra = place(ra, [2 * PH, TK])
        idxu, ra = place(ra, [2 * PH, TK], u32)
        idxf, ra = place(ra, [2 * PH, TK])
        cand, ra = place(ra, [PH, NCAND])
        crest, ra = place(ra, [PH, NCAND])
        cidx, ra = place(ra, [PH, NCAND])
        tops, ra = place(ra, [PH, TK])
        posu, ra = place(ra, [PH, TK], u32)
        posf, ra = place(ra, [PH, TK])
        esel, ra = place(ra, [PH, TK])
        gexp, ra = place(ra, [TILES, PH, TK])
        gdif, ra = place(ra, [TILES, PH, TK])
        iota50, ra = place(ra, [NCAND])
        gsum, ra = place(ra, [PH])
        grec, ra = place(ra, [PH])
        rows, pa = place(0, [SLOTS, 2 * D])
        junk, pa = place(pa, [D])
        wpg, pa = place(pa, [KC, D])
        diag, pa = place(pa, [2 * GRP, P])
        tn = junk
        wple, pa = place(pa, [2, D])
        pT, pa = place(pa, [2, S])
        gfin, pa = place(pa, [D])
        tT, pa = place(pa, [KC, P])
        tsig, pa = place(pa, [D])
        gffn = sb("gffn", [P, D])
        slot = [sb(f"slot{b}", [P, 1], i32) for b in range(2 * SLOTS)]
        dots = sb("dots", [P, 2, GRP])
        gel = sb("gel", [P, 2, GRP])
        wts = sb("wts", [P, 2, GRP])
        mx = sb("mx", [P, 32, REP])
        nm = sb("nm", [P, 32, REP])
        den = sb("den", [P, 32, REP])
        rcp = sb("rcp", [P, 32, REP])
        scl = sb("scl", [P, 32, REP])
        esk = sb("esk", [P, 32, REP])
        relb = sb("relb", [BUCKETS + 1, 2 * HEADS])
        hot, _ = place(0, [S + P])
        hot = hot[0:BUCKETS + 1, :]
        epsc = sb("epsc", [P, 1])

        psum = ctx.enter_context(nc.psum_tensor("psum", [P, 8, HALF], f32))
        ps = [psum[:, i, :] for i in range(8)]
        hp2 = psum[:, 0:2, :].rearrange("p a b -> p (a b)")
        rdram = nc.dram_tensor("bias_rows", (2 * HEADS, S + P), f32, kind="Internal").ap()

        s_xin = [sem(f"s_xin{t}") for t in range(TILES)]
        s_const = sem("s_const")
        s_rel = sem("s_rel")
        s_neg = sem("s_neg")
        s_w = [sem(f"s_w{i}") for i in range(RING)]
        s_wo = sem("s_wo")
        s_id = sem("s_id")
        s_ssq = sem("s_ssq")
        s_rstd = sem("s_rstd")
        s_xn = sem("s_xn")
        s_tr = sem("s_tr")
        s_hT = sem("s_hT")
        s_z = sem("s_z")
        s_zo = sem("s_zo")
        s_cm = sem("s_cm")
        s_rb = sem("s_rb")
        s_rbo = sem("s_rbo")
        s_rd = sem("s_rd")
        s_bias = sem("s_bias")
        s_c1 = sem("s_c1")
        s_g = sem("s_g")
        s_c2 = sem("s_c2")
        s_kc = sem("s_kc")
        s_qk = sem("s_qk")
        s_tt = sem("s_tt")
        s_nm = sem("s_nm")
        s_ex = sem("s_ex")
        s_dv = sem("s_dv")
        s_ac = sem("s_ac")
        s_sc = sem("s_sc")
        s_pp = sem("s_pp")
        s_pt = sem("s_pt")
        s_pea = sem("s_pea")
        s_ped = sem("s_ped")
        s_pv = sem("s_pv")
        s_oe = sem("s_oe")
        s_m = sem("s_m")
        s_sg = sem("s_sg")
        s_mT = sem("s_mT")
        s_o = sem("s_o")
        s_x1 = sem("s_x1")
        s_q = sem("s_q")
        s_qo = sem("s_qo")
        s_s = sem("s_s")
        s_so = sem("s_so")
        s_gd = sem("s_gd")
        s_ge = sem("s_ge")
        s_ei = sem("s_ei")
        s_tk = sem("s_tk")
        s_slot = sem("s_slot")
        s_row = [sem(f"s_row{b}") for b in range(SLOTS)]
        s_dot = sem("s_dot")
        s_gel = sem("s_gel")
        s_wt = sem("s_wt")
        s_dg = sem("s_dg")
        s_use = sem("s_use")
        s_hp = sem("s_hp")
        s_acc = sem("s_acc")
        s_tx = sem("s_tx")
        s_t1 = sem("s_t1")
        s_t2 = sem("s_t2")
        s_t3 = sem("s_t3")
        s_t4 = sem("s_t4")
        s_t5 = sem("s_t5")
        s_t6 = sem("s_t6")
        s_t7 = sem("s_t7")
        s_t8 = sem("s_t8")
        s_t9 = sem("s_t9")
        s_tail = sem("s_tail")
        s_out = sem("s_out")

        BATCH = [(n, g, br) for n in range(TILES) for g in range(GROUPS) for br in range(4)]
        SWA, SLC, WIN, CMP = range(4)

        def key_tiles(n, br):
            if br == SWA:
                return [n - 1, n] if n else [0]
            if br == CMP:
                return [0]
            return list(range(n + 1))

        PAIRS = [0]
        for n_, g_, br_ in BATCH:
            PAIRS.append(PAIRS[-1] + len(key_tiles(n_, br_)))

        def evac_counts(q):
            return q // 2 + 1, (q + 1) // 2

        def used_up(b):
            if b < ZT:
                return s_z, b + 1
            if b < B_W1:
                return s_z, ZT + TILES
            if b < B_MG:
                return s_c1, 2 * ((b - B_W1) // 4) + 2
            if b < B_WO:
                m, j = divmod(b - B_MG, 3)
                return s_m, 4 * m + (1, 2, 4)[j]
            if b < B_WQ:
                return (s_wo, b - B_WO + 1) if b < B_WQ - 1 else (s_o, 2 * TILES)
            return s_q, b - B_WQ + 1

        block = ctx.enter_context(nc.Block())

        @block.sync
        def _(sp):
            for t in range(TILES):
                sp.dma_start(xs[:, t, :], a["x"][t * P:(t + 1) * P, :]).then_inc(s_xin[t], 16)
            sp.dma_start(small[:, :], a["small"]).then_inc(s_const, 16)
            sp.dma_start(relb[0:BUCKETS, :], a["rel_bias"]).then_inc(s_rel, 16)
            sp.dma_start(hot[:, :], a["hot"]).then_inc(s_rel, 16)

            for b in range(NBLK):
                if b >= RING:
                    sp.wait_ge(*used_up(b - RING))
                sp.dma_start(ring[:, b % RING, :], a["wpack"][b, :, :]).then_inc(s_w[b % RING], 16)
                if b == 0:
                    sp.wait_ge(s_rbo, 1)
                    sp.dma_start(rdram, rbias[0:2 * HEADS, :]).then_inc(s_rd, 16)
                    sp.wait_ge(s_rd, 16)
                    for h in range(2 * HEADS):
                        w = 2 * P if h < HEADS else S
                        dst = biasA[:, h, :] if h < HEADS else biasB[:, h - HEADS, :]
                        src = bass.AP(tensor=rdram.tensor, offset=h * (S + P), ap=[[1, P], [1, w]])
                        sp.dma_start(dst, src).then_inc(s_bias, 16)
                    sp.dma_start(gffn[:, :], a["g_ffn"]).then_inc(s_const, 16)
            sp.wait_ge(s_tk, 1)
            sp.dma_start(wpg, a["w_pg"]).then_inc(s_const, 16)
            sp.dma_start(wple, a["w_ple"]).then_inc(s_const, 16)
            sp.dma_start(pT, a["pT"]).then_inc(s_const, 16)
            sp.dma_start(gfin, a["g_final"]).then_inc(s_const, 16)
            for t in range(TILES):
                sp.wait_ge(s_tail, t + 1)
                sp.dma_start(out[t * P:(t + 1) * P, :], xs[:, t, :]).then_inc(s_out, 16)
            sp.wait_ge(s_out, 16 * TILES)

        @block.gpsimd
        def _(pool):
            G.memset(zero[:, :], 0.0).then_inc(s_id, 1)
            G.memset(epsc[:, :], EPS).then_inc(s_id, 1)
            G.memset(eidx[:, TILES * COLS:], 0).then_inc(s_id, 1)
            G.memset(ident[:, :], 0.0).then_inc(s_id, 1)
            G.memset(cmask, 0.0).then_inc(s_id, 1)
            pool.wait_ge(s_id, 5)
            G.affine_select(out=ident[:, :], in_=ident[:, :], compare_op=ALU.not_equal, fill=1.0, base=0,
                            pattern=[[-1, P]], channel_multiplier=1).then_inc(s_id, 1)
            G.affine_select(out=cmask, in_=cmask, compare_op=ALU.is_ge, fill=NEG, base=-(CMP_LEN - 1),
                            pattern=[[P, TILES], [-CMP_STRIDE, NCMP]], channel_multiplier=1).then_inc(s_id, 1)
            for i, (n, g, br) in enumerate(BATCH):
                w = NCMP if br == CMP else P * len(key_tiles(n, br))
                pool.wait_ge(s_sc, i + 1)
                for r in range(REP):
                    last = G.tensor_scalar(sw[:, i % 3, r, 0:w], sw[:, i % 3, r, 0:w],
                                           scl[:, i, r:r + 1], None, ALU.mult)
                last.then_inc(s_pp, 1)
            pool.wait_ge(s_qo, 2 * PH)
            G.iota(iota50, pattern=[[1, NCAND]], base=0, channel_multiplier=0,
                   allow_small_or_imprecise_dtypes=True).then_inc(s_id, 1)
            pool.wait_ge(s_tk, 1)

            def stage(col, b):
                G.tensor_copy(slot[b][:, :], eidx[:, bass.ds(col, 1)]).then_inc(s_slot, 1)

            def gather(b):
                G.indirect_dma_start(out=rows[:, b % SLOTS, :], out_offset=None, in_=a["uv"],
                                     in_offset=bass.IndirectOffsetOnAxis(ap=slot[b][:, :], axis=0)
                                     ).then_inc(s_row[b % SLOTS], 16)

            stage(0, 0)
            for b in range(SLOTS):
                pool.wait_ge(s_slot, b + 1)
                stage(b + 1, b + 1)
                gather(b)
            body = 2 * SLOTS
            steps = TILES * COLS

            def refill(col, b):
                pool.wait_ge(s_dot, col - SLOTS + 2)
                pool.wait_ge(s_use, col - SLOTS + 1 + GRP + 1)
                pool.wait_ge(s_slot, col + 1)
                stage(col + 1, (b + 1) % body)
                gather(b)

            with pool.Fori(0, steps // body - 1) as i:
                for b in range(SLOTS, SLOTS + body):
                    refill(i * body + b, b % body)
            for b in range(SLOTS, body):
                refill(steps - body + b, b)

        @block.scalar
        def _(act):
            nac = [0]

            def after(ins):
                nac[0] += 1
                ins.then_inc(s_ac, 1)
                act.wait_ge(s_ac, nac[0])

            act.wait_ge(s_id, 2)

            def norm_rows(t, col):
                after(A.activation(hn[:, t, :], xs[:, t, :], ACT.Square, accum_out=stat[:, col + t:col + t + 1]))

            for t in range(TILES):
                act.wait_ge(s_xin[t], 16)
                norm_rows(t, 0)
            A.activation(stat[:, 4:8], stat[:, 0:4], ACT.Sqrt, scale=1.0 / D, bias=epsc[:, :]).then_inc(s_ssq, 1)
            act.wait_ge(s_const, 16)
            for k in range(KC):
                act.wait_ge(s_tr, k + 1)
                A.activation(hT[:, k, :], ps[k][:, :], ACT.Copy, scale=gmix[:, k:k + 1]).then_inc(s_hT, 1)
            for j in range(ZT + TILES):
                if j in (11, 12):
                    continue
                act.wait_ge(s_z, j + 1)
                if j < 11:
                    q = j < 4 or 5 <= j < 9
                    A.activation(qk[:, j, :], ps[j % 8][:, :], ACT.Copy, scale=SCALE if q else 1.0).then_inc(s_zo, 1)
                elif j >= ZT:
                    t = j - ZT
                    A.activation(vn[:, t, :], ps[j % 8][:, 0:NAT_COLS], ACT.Copy).then_inc(s_zo, 1)
            act.wait_ge(s_zo, 11 + TILES)
            for t in range(TILES):
                last = A.activation(gsig[:, t, :], vn[:, t, 384:408], ACT.Sigmoid)
            last.then_inc(s_zo, 1)
            for j in range(4):
                act.wait_ge(s_c1, j + 1)
                A.activation(gT[:, j // 2, j % 2, :], ps[j][:, 0:GROUPS * NCMP], ACT.Gelu_apprx_tanh).then_inc(s_g, 1)

            def pt_evac(i):
                n, g, br = BATCH[i]
                rowsn = NCMP if br == CMP else P
                for q in range(PAIRS[i], PAIRS[i + 1]):
                    if q % 2 == 0:
                        act.wait_ge(s_pt, q + 1)
                        if q >= 4:
                            act.wait_ge(s_pv, q - 3)
                        A.activation(pts[0:rowsn, q % 4, :], ps[3 + q % 3][0:rowsn, :], ACT.Copy).then_inc(s_pea, 1)

            for i in range(len(BATCH) + 2):
                if i >= 2:
                    pt_evac(i - 2)
                if i < len(BATCH):
                    n, g, br = BATCH[i]
                    w = NCMP if br == CMP else P * len(key_tiles(n, br))
                    act.wait_ge(s_nm, i + 1)
                    if br == SWA:
                        A.activation(esk[:, i, :], esk[:, i, :], ACT.Exp)
                    for r in range(REP):
                        last = A.activation(sw[:, i % 3, r, 0:w], sw[:, i % 3, r, 0:w], ACT.Exp,
                                            bias=nm[:, i, r:r + 1], accum_out=den[:, i, r:r + 1])
                    last.then_inc(s_ex, 1)
            for m in range(KC):
                for j in range(2):
                    act.wait_ge(s_m, 4 * m + j + 1)
                    if m >= 2:
                        act.wait_ge(s_mT, m - 1)
                    A.activation(sg[:, m % 2, j, :], ps[4 * (m % 2) + j][:, :], ACT.Sigmoid).then_inc(s_sg, 1)
            for t in range(TILES):
                act.wait_ge(s_x1, 2 * t + 2)
                norm_rows(t, 8)
            A.activation(stat[:, 12:16], stat[:, 8:12], ACT.Sqrt, scale=1.0 / D, bias=epsc[:, :]).then_inc(s_ssq, 1)
            for k in range(KC):
                act.wait_ge(s_tr, KC + k + 1)
                A.activation(hT[:, k, :], ps[k][:, :], ACT.Copy).then_inc(s_hT, 1)
            for j in range(2 * PH):
                act.wait_ge(s_q, j + 1)
                A.activation(qT[:, j, :], ps[j % 8][:, :], ACT.Copy).then_inc(s_qo, 1)
            for t in range(TILES):
                if t >= 2:
                    act.wait_ge(s_ei, t - 1)
                for c in range(4):
                    act.wait_ge(s_s, 4 * t + c + 1)
                    A.activation(s12[:, t % 2, 4 * c:4 * c + 4, :],
                                 ps[4 * (t % 2) + c][:, :].rearrange("p (a b) -> p a b", a=4), ACT.Copy).then_inc(s_so, 1)
                if t >= 1:
                    act.wait_ge(s_gd, t)
                    A.activation(gexp[:, t - 1, :, :], gdif[:, t - 1, :, :], ACT.Exp).then_inc(s_ge, 1)
            act.wait_ge(s_gd, TILES)
            A.activation(gexp[:, TILES - 1, :, :], gdif[:, TILES - 1, :, :], ACT.Exp).then_inc(s_ge, 1)

            act.wait_ge(s_tk, 1)
            ng = COLS // GRP
            for t in range(TILES):
                if t:
                    act.wait_ge(s_dot, t * COLS + 1)
                for c in range(2):
                    A.activation(ps[c][:, :], hn[:, t, c * HALF:(c + 1) * HALF], ACT.Copy).then_inc(s_hp, 1)
                with act.Fori(0, ng // 2) as i:
                    for e in range(2):
                        q = i * 2 + (t * ng + e)
                        act.wait_ge(s_dot, q * GRP + GRP + 1)
                        A.activation(gel[:, e, :], dots[:, e, :], ACT.Gelu_apprx_tanh).then_inc(s_gel, 1)
                        act.wait_ge(s_wt, q + 1)
                        act.wait_ge(s_use, q * GRP + 1)
                        for b in range(GRP):
                            A.activation(diag[:, e * GRP + b, :], ident[:, :], ACT.Copy, scale=wts[:, e, b:b + 1]).then_inc(s_dg, 1)
                act.wait_ge(s_tx, t + 1)
                A.activation(tsig, xs[:, t, :], ACT.Square, accum_out=stat[:, 16:17]).then_inc(s_t1, 1)
                act.wait_ge(s_t1, 2 * t + 1)
                A.activation(stat[:, 17:18], stat[:, 16:17], ACT.Sqrt, scale=1.0 / D, bias=epsc[:, :]).then_inc(s_t1, 1)
                act.wait_ge(s_t5, t + 1)
                for c in range(2):
                    A.activation(tsig[:, c * HALF:(c + 1) * HALF], ps[6 + c][:, :], ACT.Sigmoid).then_inc(s_t6, 1)
                act.wait_ge(s_t7, t + 1)
                A.activation(tsig, xs[:, t, :], ACT.Square, accum_out=stat[:, 20:21]).then_inc(s_t8, 1)
                act.wait_ge(s_t8, 2 * t + 1)
                A.activation(stat[:, 21:22], stat[:, 20:21], ACT.Sqrt, scale=1.0 / D, bias=epsc[:, :]).then_inc(s_t8, 1)

        @block.vector
        def _(dve):
            ndv = [0]

            def after(ins):
                ndv[0] += 1
                ins.then_inc(s_dv, 1)
                dve.wait_ge(s_dv, ndv[0])

            def rows_normed(first, src_col):
                dve.wait_ge(s_ssq, first)
                after(V.reciprocal(stat[:, src_col + 16:src_col + 20], stat[:, src_col:src_col + 4]))

            V.memset(relb[BUCKETS:BUCKETS + 1, :], NEG).then_inc(s_neg, 1)
            dve.wait_ge(s_rb, 1)
            V.tensor_copy(rbias[0:2 * HEADS, 0:HALF], ps[6][0:2 * HEADS, :])
            after(V.tensor_copy(rbias[0:2 * HEADS, HALF:S + P], ps[7][0:2 * HEADS, 0:P]))
            V.memset(rbias[0:HEADS, 2 * P - 1:S + P], NEG).then_inc(s_rbo, 1)
            dve.wait_ge(s_ssq, 1)
            after(V.reciprocal(stat[:, 24:28], stat[:, 4:8]))
            for t in range(TILES):
                V.tensor_scalar(hn[:, t, :], xs[:, t, :], stat[:, 24 + t:25 + t], None, ALU.mult).then_inc(s_xn, 1)
            for kv in range(2):
                j = 11 + kv
                dve.wait_ge(s_z, j + 1)
                for g in range(GROUPS):
                    src = ps[j % 8][g * DH:(g + 1) * DH, :]
                    for par in range(2):
                        v = bass.AP(tensor=src.tensor, offset=src.offset + par,
                                    ap=[list(src.ap[0]), [2, LPAIR], [CMP_STRIDE, NCMP]])
                        pos = posT[g * DH:(g + 1) * DH, par:CMP_LEN:2].unsqueeze(2).broadcast_to([DH, LPAIR, NCMP])
                        V.tensor_tensor(cm[par * DH:(par + 1) * DH, kv, :, g * NCMP:(g + 1) * NCMP], v, pos,
                                        ALU.add).then_inc(s_cm, 1)
            dve.wait_ge(s_c2, 1)
            for g in range(GROUPS):
                V.tensor_copy(kcT[g * DH:(g + 1) * DH, :], ps[4][0:DH, g * NCMP:(g + 1) * NCMP])
                last = V.tensor_copy(vcs[0:NCMP, g, :], ps[5][0:NCMP, g * DH:(g + 1) * DH])
            last.then_inc(s_kc, 1)

            def scores(i):
                n, g, br = BATCH[i]
                if i >= 3:
                    dve.wait_ge(s_pt, PAIRS[i - 2])
                if br == CMP:
                    dve.wait_ge(s_qk, 4 * i + 4)
                    src = ps[(4 * i) % 3][:, 0:REP * NCMP].rearrange("p (r c) -> p r c", r=REP)
                    mask = cmask[:, n, :].unsqueeze(1).broadcast_to([P, REP, NCMP])
                    V.tensor_tensor(sw[:, i % 3, :, 0:NCMP], src, mask, ALU.add).then_inc(s_tt, 4)
                    dve.wait_ge(s_tt, 4 * i + 4)
                    after(V.tensor_reduce(mx[:, i, :], sw[:, i % 3, :, 0:NCMP], AX.X, ALU.max))
                    V.tensor_scalar(nm[:, i, :], mx[:, i, :], NEG / 10, -1.0, ALU.max, ALU.mult).then_inc(s_nm, 1)
                    return
                w = P * len(key_tiles(n, br))
                for r in range(REP):
                    h = g * REP + r
                    bias = (biasA if br == SWA else biasB)[:, h, w - 1::-1]
                    dve.wait_ge(s_qk, 4 * i + r + 1)
                    V.tensor_tensor_reduce(out=sw[:, i % 3, r, 0:w], in0=ps[(4 * i + r) % 3][:, 0:w], in1=bias,
                                           scale=1.0, scalar=sink[:, h:h + 1] if br == SWA else NEG,
                                           op0=ALU.add, op1=ALU.max, accum_out=mx[:, i, r:r + 1]).then_inc(s_tt, 1)
                dve.wait_ge(s_tt, 4 * i + 4)
                ins = V.tensor_scalar(nm[:, i, :], mx[:, i, :], -1.0, None, ALU.mult)
                if br == SWA:
                    after(ins)
                    ins = V.tensor_tensor(esk[:, i, :], sink[:, g * REP:(g + 1) * REP], nm[:, i, :], ALU.add)
                ins.then_inc(s_nm, 1)

            def row_scales(i):
                n, g, br = BATCH[i]
                dve.wait_ge(s_ex, i + 1)
                if br == SWA:
                    after(V.tensor_tensor(den[:, i, :], den[:, i, :], esk[:, i, :], ALU.add))
                after(V.tensor_scalar(den[:, i, :], den[:, i, :], 1e-30, None, ALU.max))
                if br == SWA:
                    V.reciprocal(scl[:, i, :], den[:, i, :]).then_inc(s_sc, 1)
                    return
                after(V.reciprocal(rcp[:, i, :], den[:, i, :]))
                k = {CMP: 0, SLC: 1, WIN: 2}[br]
                V.tensor_tensor(scl[:, i, :], rcp[:, i, :], gsig[:, n, k * HEADS + g * REP:k * HEADS + (g + 1) * REP],
                                ALU.mult).then_inc(s_sc, 1)

            def pt_evac(i):
                n, g, br = BATCH[i]
                rowsn = NCMP if br == CMP else P
                for q in range(PAIRS[i], PAIRS[i + 1]):
                    if q % 2:
                        dve.wait_ge(s_pt, q + 1)
                        if q >= 4:
                            dve.wait_ge(s_pv, q - 3)
                        V.tensor_copy(pts[0:rowsn, q % 4, :], ps[3 + q % 3][0:rowsn, :]).then_inc(s_ped, 1)
                if br in (SWA, CMP):
                    dve.wait_ge(s_pv, PAIRS[i + 1])
                    dst, src = (oTA, ps[6]) if br == SWA else (oTB, ps[7])
                    src = src[0:DH, :].rearrange("p (a b t) -> p a b t", a=2, b=2)
                    for b in range(2):
                        last = V.tensor_copy(dst[b * DH:(b + 1) * DH, 2 * g:2 * g + 2, n * P:(n + 1) * P], src[:, :, b, :])
                    last.then_inc(s_oe, 1)

            dve.wait_ge(s_bias, 16 * 2 * HEADS)
            dve.wait_ge(s_id, 7)
            dve.wait_ge(s_zo, 11 + TILES + 1)
            for i in range(len(BATCH) + 2):
                if i < len(BATCH):
                    scores(i)
                if 1 <= i <= len(BATCH):
                    row_scales(i - 1)
                if i >= 2:
                    pt_evac(i - 2)
            for m in range(KC):
                b = 4 * (m % 2)
                for j in range(2):
                    dve.wait_ge(s_m, 4 * m + 3 + j)
                    dve.wait_ge(s_sg, 2 * m + j + 1)
                    last = V.tensor_tensor(sg[:, m % 2, j, :], sg[:, m % 2, j, :], ps[b + 2 + j][:, :], ALU.mult)
                after(last)
                V.tensor_tensor(mT[:, m, :], sg[:, m % 2, 0, :], sg[:, m % 2, 1, :], ALU.add).then_inc(s_mT, 1)
            for t in range(TILES):
                for c in range(2):
                    dve.wait_ge(s_o, 2 * t + c + 1)
                    V.tensor_tensor(xs[:, t, c * HALF:(c + 1) * HALF], xs[:, t, c * HALF:(c + 1) * HALF],
                                    ps[2 * t + c][:, :], ALU.add).then_inc(s_x1, 1)
            dve.wait_ge(s_ssq, 2)
            after(V.reciprocal(stat[:, 28:32], stat[:, 12:16]))
            dve.wait_ge(s_const, 32)
            for t in range(TILES):
                V.scalar_tensor_tensor(hn[:, t, :], xs[:, t, :], stat[:, 28 + t:29 + t], gffn[:, :],
                                       ALU.mult, ALU.mult).then_inc(s_xn, 1)
            dve.wait_ge(s_id, 8)
            for t in range(TILES):
                dve.wait_ge(s_so, 4 * t + 4)
                sc = s12[:, t % 2, :, :]
                if t:
                    dve.wait_ge(s_ei, t)
                for j in range(2 * PH):
                    last = V.max(vals[:, j, 0:8], sc[:, j, :])
                after(last)
                for j in range(2 * PH):
                    V.max_index(idxu[:, j, 0:8], vals[:, j, 0:8], sc[:, j, :])
                    last = V.match_replace(rest[:, j, :], vals[:, j, 0:8], sc[:, j, :], -3e38)
                after(last)
                for j in range(2 * PH):
                    last = V.max(vals[:, j, 8:16], rest[:, j, :])
                after(last)
                for j in range(2 * PH):
                    last = V.max_index(idxu[:, j, 8:16], vals[:, j, 8:16], rest[:, j, :])
                after(last)
                after(V.tensor_copy(idxf, idxu))
                i4 = idxf.rearrange("p (h s) k -> p h s k", s=2)
                v4 = vals.rearrange("p (h s) k -> p h s k", s=2)
                after(V.tensor_scalar(i4[:, :, 0, :], i4[:, :, 0, :], float(PK), None, ALU.mult))
                for src, dst in ((v4, cand), (i4, cidx)):
                    off = 0
                    for a0, na, nb in RUNS:
                        d = dst[:, :, off:off + na * nb].rearrange("p h (x y) -> p h x y", x=na)
                        last = V.tensor_tensor(d, src[:, :, 0, a0:a0 + na].unsqueeze(3).broadcast_to([P, PH, na, nb]),
                                               src[:, :, 1, 0:nb].unsqueeze(2).broadcast_to([P, PH, na, nb]), ALU.add)
                        off += na * nb
                after(last)
                for h in range(PH):
                    last = V.max(tops[:, h, 0:8], cand[:, h, :])
                after(last)
                for h in range(PH):
                    V.max_index(posu[:, h, 0:8], tops[:, h, 0:8], cand[:, h, :])
                    last = V.match_replace(crest[:, h, :], tops[:, h, 0:8], cand[:, h, :], -3e38)
                after(last)
                for h in range(PH):
                    last = V.max(tops[:, h, 8:16], crest[:, h, :])
                after(last)
                for h in range(PH):
                    last = V.max_index(posu[:, h, 8:16], tops[:, h, 8:16], crest[:, h, :])
                V.tensor_tensor(gdif[:, t, :, :], tops, tops[:, :, 0:1].broadcast_to([P, PH, TK]),
                                ALU.subtract).then_inc(s_gd, 1)
                dve.wait_ge(s_gd, t + 1)
                after(V.tensor_copy(posf, posu))
                e4 = eqt.rearrange("p (h k) c -> p h k c", h=PH)
                if t == 0:
                    dve.wait_ge(s_s, 4 * TILES)
                after(V.tensor_tensor(e4, iota50.unsqueeze(1).unsqueeze(1).broadcast_to([P, PH, TK, NCAND]),
                                      posf.unsqueeze(3).broadcast_to([P, PH, TK, NCAND]), ALU.is_equal))
                after(V.tensor_tensor(e4, e4, cidx.unsqueeze(2).broadcast_to([P, PH, TK, NCAND]), ALU.mult))
                after(V.tensor_reduce(esel.rearrange("p h k -> p (h k)"), eqt, AX.X, ALU.add))
                V.tensor_copy(eidx[:, t * COLS:(t + 1) * COLS], esel.rearrange("p h k -> p (h k)")).then_inc(s_ei, 1)
                dve.wait_ge(s_ge, t + 1)
                after(V.tensor_reduce(gsum, gexp[:, t, :, :], AX.X, ALU.add))
                after(V.reciprocal(grec, gsum))
                last = V.tensor_tensor(gate[:, t * COLS:(t + 1) * COLS].rearrange("p (h k) -> p h k", h=PH),
                                       gexp[:, t, :, :], grec.unsqueeze(2).broadcast_to([P, PH, TK]), ALU.mult)
                if t == TILES - 1:
                    last.then_inc(s_tk, 1)
                else:
                    after(last)

            dve.wait_ge(s_tk, 1)
            V.memset(dots[:, :, :], 0.0).then_inc(s_dot, 1)
            ng = COLS // GRP
            for t in range(TILES):
                dve.wait_ge(s_hp, 2 * t + 2)
                with dve.Fori(0, ng // 2) as i:
                    for e in range(2):
                        q = i * 2 + (t * ng + e)
                        for b in range(GRP):
                            n = q * GRP + b
                            s = e * GRP + b
                            dve.wait_ge(s_dot, n + 1)
                            dve.wait_ge(s_row[s], i * 16 + (t * (COLS // SLOTS) + 1) * 16)
                            V.tensor_tensor_reduce(out=junk, in0=hp2[:, :], in1=rows[:, s, 0:D],
                                                   scale=1.0, scalar=0.0, op0=ALU.mult, op1=ALU.add,
                                                   accum_out=dots[:, e, b:b + 1]).then_inc(s_dot, 1)
                        dve.wait_ge(s_gel, q + 1)
                        V.tensor_tensor(wts[:, e, :], gel[:, e, :],
                                        gate[:, bass.ds(i * (2 * GRP) + (t * COLS + e * GRP), GRP)],
                                        ALU.mult).then_inc(s_wt, 1)
                dve.wait_ge(s_acc, t + 1)
                for c in range(2):
                    last = V.tensor_copy(xs[:, t, c * HALF:(c + 1) * HALF], ps[2 + c][:, :])
                last.then_inc(s_tx, 1)
                dve.wait_ge(s_t1, 2 * t + 2)
                after(V.reciprocal(stat[:, 18:19], stat[:, 17:18]))
                V.tensor_scalar(tn, xs[:, t, :], stat[:, 18:19], None, ALU.mult).then_inc(s_t2, 1)
                for c in range(2):
                    dve.wait_ge(s_t3, 2 * t + c + 1)
                    V.tensor_tensor(tT[:, 4 * c:4 * c + 4, :], ps[4 + c][:, :].rearrange("p (a b) -> p a b", a=4),
                                    gple[:, 4 * c:4 * c + 4].unsqueeze(2).broadcast_to([P, 4, P]), ALU.mult).then_inc(s_t4, 1)
                dve.wait_ge(s_t6, 2 * t + 2)
                for c in range(2):
                    last = V.tensor_tensor(tsig[:, c * HALF:(c + 1) * HALF], tsig[:, c * HALF:(c + 1) * HALF],
                                           ps[4 + c][:, :], ALU.mult)
                after(last)
                V.tensor_tensor(xs[:, t, :], xs[:, t, :], tsig, ALU.add).then_inc(s_t7, 1)
                dve.wait_ge(s_t8, 2 * t + 2)
                after(V.reciprocal(stat[:, 22:23], stat[:, 21:22]))
                V.scalar_tensor_tensor(xs[:, t, :], xs[:, t, :], stat[:, 22:23], gfin[:, :],
                                       ALU.mult, ALU.mult).then_inc(s_tail, 1)

        @block.tensor
        def _(pe):
            def arrive(b):
                pe.wait_ge(s_w[b % RING], 16 * (b // RING + 1))

            def blk(b):
                return ring[:, b % RING, :]

            pe.wait_ge(s_rel, 32)
            pe.wait_ge(s_id, 7)
            pe.wait_ge(s_neg, 1)
            T.matmul(ps[6][0:2 * HEADS, :], relb[:, :], hot[:, 0:HALF], start=True, stop=True)
            T.matmul(ps[7][0:2 * HEADS, 0:P], relb[:, :], hot[:, HALF:S + P], start=True, stop=True).then_inc(s_rb, 1)
            pe.wait_ge(s_rbo, 1)

            def transpose_rows(first):
                pe.wait_ge(s_xn, first + TILES)
                for k in range(KC):
                    for t in range(TILES):
                        last = T.transpose(ps[k][:, t * P:(t + 1) * P], hn[:, t, k * P:(k + 1) * P], ident[:, :])
                    last.then_inc(s_tr, 1)

            transpose_rows(0)
            pe.wait_ge(s_hT, KC)
            for j in range(ZT):
                arrive(j)
                if j >= 8:
                    pe.wait_ge(s_zo, j - 7)
                for k in range(KC):
                    last = T.matmul(ps[j % 8], blk(j)[:, k * P:(k + 1) * P], hT[:, k, :],
                                    start=(k == 0), stop=(k == KC - 1))
                last.then_inc(s_z, 1)
            for b in range(NATB):
                arrive(B_NAT + b)
            for t in range(TILES):
                j = ZT + t
                pe.wait_ge(s_zo, j - 7)
                for k in range(KC):
                    w = blk(B_NAT + k // 2)[:, (k % 2) * HALF:(k % 2) * HALF + NAT_COLS]
                    last = T.matmul(ps[j % 8][:, 0:NAT_COLS], hT[:, k, t * P:(t + 1) * P], w,
                                    start=(k == 0), stop=(k == KC - 1))
                last.then_inc(s_z, 1)
            for kv in range(2):
                pe.wait_ge(s_cm, 4 * kv + 4)
                if kv == 0:
                    pe.wait_ge(s_zo, 11 + TILES)
                for b in range(4):
                    arrive(B_W1 + 4 * kv + b)
                for hb in range(2):
                    for l in range(LPAIR):
                        w = blk(B_W1 + 4 * kv + l // 4)[:, (l % 4) * CMP_HID + hb * P:(l % 4) * CMP_HID + (hb + 1) * P]
                        last = T.matmul(ps[2 * kv + hb][:, 0:GROUPS * NCMP], w, cm[:, kv, l, :],
                                        start=(l == 0), stop=(l == LPAIR - 1))
                    last.then_inc(s_c1, 1)
            pe.wait_ge(s_g, 4)
            for hb in range(2):
                T.matmul(ps[4][0:DH, 0:GROUPS * NCMP], w2[:, 0, hb, :], gT[:, 0, hb, :], start=(hb == 0), stop=(hb == 1))
            for g in range(GROUPS):
                for hb in range(2):
                    last = T.matmul(ps[5][0:NCMP, g * DH:(g + 1) * DH], gT[:, 1, hb, g * NCMP:(g + 1) * NCMP],
                                    w2[:, 1, hb, :], start=(hb == 0), stop=(hb == 1))
            last.then_inc(s_c2, 1)

            def queries_keys(i):
                n, g, br = BATCH[i]
                half = slice(g * DH, (g + 1) * DH)
                kts = key_tiles(n, br)
                w = P * len(kts)
                for r in range(REP):
                    u = 4 * i + r
                    q = qk[half, r if br == SWA else 5 + r, n * P:(n + 1) * P]
                    if u >= 3 and (br != CMP or r == 0):
                        pe.wait_ge(s_tt, u - 2)
                    if br == CMP:
                        T.matmul(ps[(4 * i) % 3][:, r * NCMP:(r + 1) * NCMP], q, kcT[half, :],
                                 start=True, stop=True).then_inc(s_qk, 1)
                    else:
                        k = qk[half, {SWA: 4, SLC: 9, WIN: 10}[br], kts[0] * P:kts[0] * P + w]
                        T.matmul(ps[u % 3][:, 0:w], q, k, start=True, stop=True).then_inc(s_qk, 1)

            def weigh_values(i):
                n, g, br = BATCH[i]
                kts = key_tiles(n, br)
                keys = NCMP if br == CMP else P
                pe.wait_ge(s_pp, i + 1)

                def turn(x):
                    q = PAIRS[i] + x
                    if q >= 3:
                        ev, od = evac_counts(q - 3)
                        pe.wait_ge(s_pea, ev) if (q - 3) % 2 == 0 else pe.wait_ge(s_ped, od)
                    for r in range(REP):
                        last = T.transpose(ps[3 + q % 3][0:keys, r * P:(r + 1) * P],
                                           sw[:, i % 3, r, x * P:x * P + keys], ident[:, :])
                    last.then_inc(s_pt, 1)

                def apply(x):
                    q = PAIRS[i] + x
                    ev, od = evac_counts(q)
                    pe.wait_ge(s_pea, ev) if q % 2 == 0 else pe.wait_ge(s_ped, od)
                    if br == CMP:
                        val = vcs[0:NCMP, g, :]
                    else:
                        c = {SWA: 0, SLC: 128, WIN: 256}[br] + g * DH
                        val = vn[:, kts[x], c:c + DH]
                    T.matmul(ps[6 if br == SWA else 7][0:DH, :], val, pts[0:keys, q % 4, :],
                             start=(x == 0 and br in (SWA, SLC)),
                             stop=(x == len(kts) - 1 and br in (SWA, CMP))).then_inc(s_pv, 1)

                og = 2 * (n * GROUPS + g)
                turn(0)
                if br in (SWA, SLC) and og:
                    pe.wait_ge(s_oe, og - 1 if br == SWA else og)
                for x in range(1, len(kts)):
                    turn(x)
                    apply(x - 1)
                apply(len(kts) - 1)

            pe.wait_ge(s_kc, 1)
            for i in range(len(BATCH) + 2):
                if i < len(BATCH):
                    queries_keys(i)
                if i >= 2:
                    weigh_values(i - 2)
            pe.wait_ge(s_oe, 2 * TILES * GROUPS)
            for m in range(KC):
                base = 4 * (m % 2)
                for j in range(2):
                    b = B_MG + 3 * m + j
                    arrive(b)
                    if m >= 2:
                        pe.wait_ge(s_mT, m - 1)
                    for k in range(KC):
                        last = T.matmul(ps[base + j], blk(b)[:, k * P:(k + 1) * P], hT[:, k, :],
                                        start=(k == 0), stop=(k == KC - 1))
                    last.then_inc(s_m, 1)
                b = B_MG + 3 * m + 2
                arrive(b)
                for j, oT in enumerate((oTA, oTB)):
                    for c in range(4):
                        last = T.matmul(ps[base + 2 + j], blk(b)[:, (4 * j + c) * P:(4 * j + c + 1) * P], oT[:, c, :],
                                        start=(c == 0), stop=(c == 3))
                    last.then_inc(s_m, 1)
            for k in range(KC):
                arrive(B_WO + k)
                pe.wait_ge(s_mT, KC if k == 0 else KC)
                for t in range(TILES):
                    for c in range(2):
                        last = T.matmul(ps[2 * t + c], mT[:, k, t * P:(t + 1) * P],
                                        blk(B_WO + k)[:, c * HALF:(c + 1) * HALF], start=(k == 0), stop=(k == KC - 1))
                        if k == KC - 1:
                            last.then_inc(s_o, 1)
                if k < KC - 1:
                    last.then_inc(s_wo, 1)
            transpose_rows(TILES)
            pe.wait_ge(s_hT, 2 * KC)
            for j in range(2 * PH):
                arrive(B_WQ + j)
                if j >= 8:
                    pe.wait_ge(s_qo, j - 7)
                for k in range(KC):
                    last = T.matmul(ps[j % 8], blk(B_WQ + j)[:, k * P:(k + 1) * P], hT[:, k, :],
                                    start=(k == 0), stop=(k == KC - 1))
                last.then_inc(s_q, 1)
            pe.wait_ge(s_qo, 2 * PH)
            for t in range(TILES):
                if t >= 2:
                    pe.wait_ge(s_so, 4 * (t - 1))
                for c in range(4):
                    for j in range(4 * c, 4 * c + 4):
                        last = T.matmul(ps[4 * (t % 2) + c][:, (j % 4) * PK:(j % 4 + 1) * PK], qT[:, j, t * P:(t + 1) * P],
                                        pkeys[:, j % 2, :], start=True, stop=True)
                    last.then_inc(s_s, 1)
            pe.wait_ge(s_tk, 1)
            ng = COLS // GRP

            def open_sum(t):
                if t:
                    pe.wait_ge(s_tx, t)
                for c in range(2):
                    last = T.matmul(ps[2 + c], ident[:, :], xs[:, t, c * HALF:(c + 1) * HALF], start=True, stop=False)
                return last

            open_sum(0).then_inc(s_use, GRP + 1)
            for t in range(TILES):
                with pe.Fori(0, ng // 2) as i:
                    for s in range(SLOTS):
                        pe.wait_ge(s_dg, i * SLOTS + (t * COLS + s + 1))
                        for c in range(2):
                            last = T.matmul(ps[2 + c], diag[:, s, :], rows[:, s, D + c * HALF:D + (c + 1) * HALF],
                                            start=False, stop=False)
                        last.then_inc(s_use, 1)
                for c in range(2):
                    last = T.matmul(ps[2 + c], zero[:, :], xs[:, t, c * HALF:(c + 1) * HALF], start=False, stop=True)
                last.then_inc(s_acc, 1)
                if t < TILES - 1:
                    open_sum(t + 1)
                pe.wait_ge(s_t2, t + 1)
                if t:
                    pe.wait_ge(s_t7, t)
                for c in range(2):
                    for k in range(4):
                        last = T.transpose(ps[4 + c][:, k * P:(k + 1) * P], tn[:, (4 * c + k) * P:(4 * c + k + 1) * P], ident[:, :])
                    last.then_inc(s_t3, 1)
                pe.wait_ge(s_const, 16 * 6)
                pe.wait_ge(s_t4, 2 * t + 2)
                for c in range(2):
                    for k in range(KC):
                        T.matmul(ps[6 + c], tT[:, k, :], wpg[:, k, c * HALF:(c + 1) * HALF], start=(k == 0), stop=(k == KC - 1))
                for c in range(2):
                    for k in range(2):
                        last = T.matmul(ps[4 + c], pT[:, k, t * P:(t + 1) * P], wple[:, k, c * HALF:(c + 1) * HALF],
                                        start=(k == 0), stop=(k == 1))
                last.then_inc(s_t5, 1)


OUT_SHAPE = (1, S, D)


def lay_out(i):
    f = {k: np.asarray(v) for k, v in i.items()}
    w_in = f["w_in"][0]
    ar = np.arange

    def by_chunk(w, cols):
        return w[:, cols].reshape(KC, P, len(cols)).transpose(1, 0, 2).reshape(P, -1)

    q_a, k_a, v_a, q_b = 0, 512, 640, 768
    k_c, v_c, k_s, v_s, k_w, v_w, b_g, m_g = 1280, 1408, 1536, 1664, 1792, 1920, 2048, 2072
    pair = lambda base, r: np.concatenate([ar(DH) + base + r * DH, ar(DH) + base + (r + REP) * DH])
    run = lambda base: ar(P) + base
    zcols = [pair(q_a, r) for r in range(REP)] + [run(k_a)] + [pair(q_b, r) for r in range(REP)]
    zcols += [run(k_s), run(k_w), run(k_c), run(v_c)]
    blocks = [by_chunk(w_in, c) for c in zcols]
    nat = np.concatenate([run(v_a), run(v_s), run(v_w), ar(3 * HEADS) + b_g])
    wn = np.zeros((P, KC, HALF), np.float32)
    wn[:, :, :NAT_COLS] = by_chunk(w_in, nat).reshape(P, KC, NAT_COLS)
    blocks += [wn[:, 2 * b:2 * b + 2].reshape(P, D) for b in range(NATB)]
    for w in ("cmp_k_w1", "cmp_v_w1"):
        w1 = f[w][0].reshape(LPAIR, P, CMP_HID)
        blocks += [w1[4 * b:4 * b + 4].transpose(1, 0, 2).reshape(P, D) for b in range(4)]
    for m in range(KC):
        blocks += [by_chunk(w_in, run(m_g + m * P)), by_chunk(w_in, run(m_g + D + m * P))]
        up = np.concatenate([f["w_up_a"][0], f["w_up_b"][0]])
        blocks.append(by_chunk(up, run(m * P)))
    blocks += [f["w_o"][0][k * P:(k + 1) * P] for k in range(KC)]
    blocks += [by_chunk(f["peer_wq"][0], run(j * P)) for j in range(2 * PH)]
    pos = f["cmp_pos"][0].T
    w2 = np.stack([f["cmp_k_w2"][0].reshape(2, P, DH), f["cmp_v_w2"][0].reshape(2, P, DH)])
    small = np.concatenate([
        f["g_mix"][0].reshape(KC, P).T, f["g_ple"][0].reshape(KC, P).T, np.concatenate([pos, pos]),
        np.broadcast_to(f["a_sink"][0].reshape(1, HEADS), (P, HEADS)),
        w2.transpose(2, 0, 1, 3).reshape(P, -1),
        f["peer_k1"][0].T, f["peer_k2"][0].T], axis=1)
    rel = f["rel_bias"]
    return {
        "x": f["x"][0],
        "small": small,
        "rel_bias": rel,
        "hot": bucket_onehot(),
        "wpack": np.stack(blocks),
        "g_ffn": np.broadcast_to(f["g_ffn"][0][None], (P, D)),
        "g_final": np.broadcast_to(f["g_final"][None], (P, D)),
        "pT": f["p"][0, 0].T.reshape(2, P, S).transpose(1, 0, 2),
        "w_ple": f["w_ple"][0].reshape(2, P, D).transpose(1, 0, 2),
        "w_pg": f["w_ple_gate"][0].reshape(KC, P, D).transpose(1, 0, 2),
        "uv": np.concatenate([f["peer_u"][0], f["peer_v"][0]], axis=1),
    }


def kernel(**inputs):
    import concourse.bacc as bacc
    from concourse.bass_utils import run_bass_kernel_spmd

    nc = bacc.Bacc("TRN2", target_bir_lowering=False, num_devices=1)
    arrays, aps = {}, {}
    for name, v in lay_out(inputs).items():
        v = np.ascontiguousarray(v)
        arrays[f"in_{name}"] = v
        aps[name] = nc.dram_tensor(f"in_{name}", v.shape, mybir.dt.from_np(v.dtype), kind="ExternalInput").ap()
    out = nc.dram_tensor("out", (S, D), mybir.dt.float32, kind="ExternalOutput").ap()
    build(nc, aps, out)
    got = run_bass_kernel_spmd(nc, [arrays], core_ids=[0])
    return got.results[0]["out"].reshape(OUT_SHAPE)
```

```python
import math
from contextlib import ExitStack

import numpy as np

import concourse.bass as bass
from concourse import mybir

D = 1024
S = 512
P = 128
TILES = S // P
KC = D // P
HALF = 512
DH = 64
HEADS = 8
GROUPS = 2
REP = HEADS // GROUPS
BUCKETS, MAX_EXACT, MAX_DIST = 32, 16, 128
CMP_LEN, CMP_STRIDE, CMP_HID = 32, 16, 256
NCMP = S // CMP_STRIDE - CMP_LEN // CMP_STRIDE + 1
LPAIR = CMP_LEN // 2
PK = 128
PH = 8
TK = 16
COLS = PH * TK
PLE = 256
EPS = 1e-6
NEG = -1e30
SCALE = DH ** -0.5

RUNS = [(0, 1, 16), (1, 1, 8), (2, 1, 5), (3, 1, 4), (4, 1, 3), (5, 3, 2), (8, 8, 1)]
NCAND = sum(na * nb for _, na, nb in RUNS)

ZT = 13
NAT_COLS = 3 * 128 + 24
NATB = 4
B_W1 = ZT
B_NAT = B_W1 + 8
B_MG = B_NAT + NATB
B_WO = B_MG + 3 * KC
B_WQ = B_WO + KC
B_WQ2 = B_WQ + 2 * PH
NBLK = B_WQ2 + 2 * PH
RING = 6

SLOTS = 8
GRP = 4
GROUPS_T = COLS // GRP
SEGS = (16, 8, 8, 8)
assert SLOTS == 2 * GRP and all(GROUPS_T % (2 * n) == 0 for n in SEGS)


def bucket_onehot():
    width = S + P
    out = np.zeros((BUCKETS + 1, width), np.float32)
    for y in range(width):
        dist = y - (P - 1)
        if dist < 0:
            out[BUCKETS, y] = 1.0
            continue
        b = dist
        if dist >= MAX_EXACT:
            b = MAX_EXACT + int(math.log(dist / MAX_EXACT) / math.log(MAX_DIST / MAX_EXACT) * (BUCKETS - MAX_EXACT))
            b = min(b, BUCKETS - 1)
        out[b, y] = 1.0
    return out


def build(nc, a, out):
    f32, i32, u32 = mybir.dt.float32, mybir.dt.int32, mybir.dt.uint32
    ALU, ACT, AX = mybir.AluOpType, mybir.ActivationFunctionType, mybir.AxisListType
    V, T, A, G = nc.vector, nc.tensor, nc.scalar, nc.gpsimd
    ctx = ExitStack()
    with ctx:
        def sb(name, shape, dt=f32):
            return ctx.enter_context(nc.sbuf_tensor(name, shape, dt))

        def sem(name):
            return ctx.enter_context(nc.semaphore(name))

        xs = sb("xs", [P, TILES, D])
        hn = sb("hn", [P, TILES, D])
        ring = sb("ring", [P, RING, D])
        ident = sb("ident", [P, P])
        zero = sb("zero", [P, P])
        small = sb("small", [P, 8 + 8 + CMP_LEN + 8 + 256 + 256])
        gmix, gple = small[:, 0:8], small[:, 8:16]
        posT = small[:, 16:48]
        sink = small[:, 48:56]
        w2 = small[:, 56:312].rearrange("p (v h d) -> p v h d", v=2, h=2)
        pkeys = small[:, 312:568].rearrange("p (h n) -> p h n", h=2)
        eidx = sb("eidx", [P, TILES * COLS + 1], i32)
        gate = sb("gate", [P, TILES * COLS])
        stat = sb("stat", [P, 64])
        ARENA = 34420
        ar = sb("arena", [P, ARENA])

        def place(start, shape, dt=None):
            n = int(np.prod(shape))
            assert start + n <= ARENA, (start, shape)
            v = ar[:, start:start + n]
            if dt is not None:
                v = v.bitcast(dt)
            if len(shape) == 2:
                v = v.rearrange("p (a b) -> p a b", a=shape[0])
            if len(shape) == 3:
                v = v.rearrange("p (a b c) -> p a b c", a=shape[0], b=shape[1])
            return v, start + n

        at = 0
        hT, at = place(at, [KC, S])
        at_q = at
        qk, at = place(at, [11, S])
        vn, at = place(at, [TILES, NAT_COLS])
        gsig, at = place(at, [TILES, 24])
        biasB, at = place(at, [HEADS, S])
        biasA, at = place(at, [HEADS, 2 * P])
        sw, at = place(at, [3, REP, S])
        pts, at = place(at, [4, S])
        cm, at = place(at, [2, LPAIR, GROUPS * NCMP])
        gT, at = place(at, [2, 2, GROUPS * NCMP])
        kcT, at = place(at, [NCMP])
        vcs, at = place(at, [GROUPS, DH])
        cmask, at = place(at, [TILES, NCMP])
        oTA, at = place(at, [4, S])
        oTB, at = place(at, [4, S])
        mx, at = place(at, [32, REP])
        nm, at = place(at, [32, REP])
        den, at = place(at, [32, REP])
        rcp, at = place(at, [32, REP])
        scl, at = place(at, [32, REP])
        esk, at = place(at, [32, REP])
        rbias, _ = place(at_q + 11 * S + TILES * NAT_COLS + TILES * 24 + 6 * S * 2, [S + P])
        mT, _ = place(at_q, [KC, S])
        sg, _ = place(at_q + 11 * S + TILES * NAT_COLS + TILES * 24, [2, 2, S])
        s12_0, ra = place(at_q, [2 * PH, PK])
        scr_0, ra = place(ra, [D])
        assert ra <= SLOTS * 2 * D
        ringf = ring.rearrange("p a b -> p (a b)")
        s12 = [s12_0] + [ringf[:, i * 2 * PH * PK:(i + 1) * 2 * PH * PK].rearrange("p (j n) -> p j n", j=2 * PH)
                         for i in range(TILES - 1)]
        rows, pa = place(0, [SLOTS, 2 * D])
        junk, pa = place(pa, [D])
        diag, pa = place(pa, [2 * GRP, P])
        late = pa
        wpg, pa = place(pa, [KC, D])
        tT, pa = place(pa, [KC, P])
        tsig, pa = place(pa, [D])
        wple, pa = place(pa, [2, D])
        pT, pa = place(pa, [2, S])
        h2T, qa = place(late, [KC, S])
        qT0, qa = place(qa, [2 * PH, P])
        qT1, qa = place(qa, [2 * PH, S - P])
        assert qa <= pa
        vals, pa = place(pa, [2 * PH, TK])
        idxu, pa = place(pa, [2 * PH, TK], u32)
        idxf, pa = place(pa, [2 * PH, TK])
        cand, pa = place(pa, [PH, NCAND])
        crest, pa = place(pa, [PH, NCAND])
        cidx, pa = place(pa, [PH, NCAND])
        tops, pa = place(pa, [PH, TK])
        posu, pa = place(pa, [PH, TK], u32)
        posf, pa = place(pa, [PH, TK])
        esel, pa = place(pa, [PH, TK])
        gdif, pa = place(pa, [PH, TK])
        iota50, pa = place(pa, [NCAND])
        gsum, pa = place(pa, [PH])
        grec, pa = place(pa, [PH])
        gffn = sb("gffn", [P, D])
        gfin = gffn
        slot = [sb(f"slot{b}", [P, 1], i32) for b in range(2 * SLOTS)]
        dots = sb("dots", [P, 2, GRP])
        gel = sb("gel", [P, 2, GRP])
        wts = sb("wts", [P, 2, GRP])
        relb = sb("relb", [BUCKETS + 1, 2 * HEADS])
        hot, _ = place(0, [S + P])
        hot = hot[0:BUCKETS + 1, :]
        epsc = sb("epsc", [P, 1])

        psum = ctx.enter_context(nc.psum_tensor("psum", [P, 8, HALF], f32))
        ps = [psum[:, i, :] for i in range(8)]
        hp2 = psum[:, 0:2, :].rearrange("p a b -> p (a b)")
        rdram = nc.dram_tensor("bias_rows", (2 * HEADS, S + P), f32, kind="Internal").ap()

        s_xin = [sem(f"s_xin{t}") for t in range(TILES)]
        s_const = sem("s_const")
        s_rel = sem("s_rel")
        s_neg = sem("s_neg")
        s_w = [sem(f"s_w{i}") for i in range(RING)]
        s_wo = sem("s_wo")
        s_id = sem("s_id")
        s_ssq = sem("s_ssq")
        s_rstd = sem("s_rstd")
        s_xn = sem("s_xn")
        s_tr = sem("s_tr")
        s_hT = sem("s_hT")
        s_z = sem("s_z")
        s_zo = sem("s_zo")
        s_cm = sem("s_cm")
        s_rb = sem("s_rb")
        s_rbo = sem("s_rbo")
        s_rd = sem("s_rd")
        s_bias = sem("s_bias")
        s_c1 = sem("s_c1")
        s_g = sem("s_g")
        s_c2 = sem("s_c2")
        s_kc = sem("s_kc")
        s_qk = sem("s_qk")
        s_tt = sem("s_tt")
        s_nm = sem("s_nm")
        s_ex = sem("s_ex")
        s_dv = sem("s_dv")
        s_ac = sem("s_ac")
        s_sc = sem("s_sc")
        s_pp = sem("s_pp")
        s_pt = sem("s_pt")
        s_pea = sem("s_pea")
        s_ped = sem("s_ped")
        s_pv = sem("s_pv")
        s_oe = sem("s_oe")
        s_m = sem("s_m")
        s_sg = sem("s_sg")
        s_mT = sem("s_mT")
        s_o = sem("s_o")
        s_x1 = sem("s_x1")
        s_q = sem("s_q")
        s_qo = sem("s_qo")
        s_s = sem("s_s")
        s_so = sem("s_so")
        s_gd = sem("s_gd")
        s_ge = sem("s_ge")
        s_ei = sem("s_ei")
        s_tk = sem("s_tk")
        s_slot = sem("s_slot")
        s_row = [sem(f"s_row{b}") for b in range(SLOTS)]
        s_dot = sem("s_dot")
        s_gel = sem("s_gel")
        s_wt = sem("s_wt")
        s_dg = sem("s_dg")
        s_use = sem("s_use")
        s_hp = sem("s_hp")
        s_acc = sem("s_acc")
        s_tx = sem("s_tx")
        s_t1 = sem("s_t1")
        s_t2 = sem("s_t2")
        s_t3 = sem("s_t3")
        s_t4 = sem("s_t4")
        s_t5 = sem("s_t5")
        s_t6 = sem("s_t6")
        s_t7 = sem("s_t7")
        s_t8 = sem("s_t8")
        s_t9 = sem("s_t9")
        s_tail = sem("s_tail")
        s_out = sem("s_out")

        BATCH = [(n, g, br) for n in range(TILES) for g in range(GROUPS) for br in range(4)]
        SWA, SLC, WIN, CMP = range(4)

        def key_tiles(n, br):
            if br == SWA:
                return [n - 1, n] if n else [0]
            if br == CMP:
                return [0]
            return list(range(n + 1))

        PAIRS = [0]
        for n_, g_, br_ in BATCH:
            PAIRS.append(PAIRS[-1] + len(key_tiles(n_, br_)))

        def evac_counts(q):
            return q // 2 + 1, (q + 1) // 2

        def segment(t, seg):
            groups = GROUPS_T // SEGS[t]
            return t * GROUPS_T + seg * groups, groups // 2

        def used_up(b):
            if b < ZT:
                return s_z, b + 1
            if b < B_NAT:
                return s_c1, 2 * ((b - B_W1) // 4) + 2
            if b < B_MG:
                return s_z, ZT + TILES
            if b < B_WO:
                m, j = divmod(b - B_MG, 3)
                return s_m, 4 * m + (1, 2, 4)[j]
            if b < B_WQ:
                return (s_wo, b - B_WO + 1) if b < B_WQ - 1 else (s_o, 2 * TILES)
            return s_q, b - B_WQ + 1

        EMBED = (6, 6, 6, 2)
        SCORE_SEGS = (7, 9, 11)

        block = ctx.enter_context(nc.Block())

        @block.sync
        def _(sp):
            for t in range(TILES):
                sp.dma_start(xs[:, t, :], a["x"][t * P:(t + 1) * P, :]).then_inc(s_xin[t], 16)
            sp.dma_start(small[:, :], a["small"]).then_inc(s_const, 16)
            sp.dma_start(relb[0:BUCKETS, :], a["rel_bias"]).then_inc(s_rel, 16)
            sp.dma_start(hot[:, :], a["hot"]).then_inc(s_rel, 16)

            for b in range(NBLK):
                if b >= RING:
                    sp.wait_ge(*used_up(b - RING))
                src = b if b < B_WQ2 else b - 2 * PH
                sp.dma_start(ring[:, b % RING, :], a["wpack"][src, :, :]).then_inc(s_w[b % RING], 16)
                if b == 0:
                    sp.wait_ge(s_rbo, 1)
                    sp.dma_start(rdram, rbias[0:2 * HEADS, :]).then_inc(s_rd, 16)
                    sp.wait_ge(s_rd, 16)
                    for h in range(2 * HEADS):
                        w = 2 * P if h < HEADS else S
                        dst = biasA[:, h, :] if h < HEADS else biasB[:, h - HEADS, :]
                        src = bass.AP(tensor=rdram.tensor, offset=h * (S + P), ap=[[1, P], [1, w]])
                        sp.dma_start(dst, src).then_inc(s_bias, 16)
                    sp.dma_start(gffn[:, :], a["g_ffn"]).then_inc(s_const, 16)
            sp.wait_ge(s_s, 4 * TILES)
            sp.dma_start(wpg, a["w_pg"]).then_inc(s_const, 16)
            sp.dma_start(wple, a["w_ple"]).then_inc(s_const, 16)
            sp.dma_start(pT, a["pT"]).then_inc(s_const, 16)
            sp.dma_start(gfin[:, :], a["g_final"]).then_inc(s_const, 16)
            for t in range(TILES):
                sp.wait_ge(s_tail, t + 1)
                sp.dma_start(out[t * P:(t + 1) * P, :], xs[:, t, :]).then_inc(s_out, 16)
            sp.wait_ge(s_out, 16 * TILES)

        @block.gpsimd
        def _(pool):
            G.memset(zero[:, :], 0.0).then_inc(s_id, 1)
            G.memset(epsc[:, :], EPS).then_inc(s_id, 1)
            G.memset(eidx[:, TILES * COLS:], 0).then_inc(s_id, 1)
            G.memset(ident[:, :], 0.0).then_inc(s_id, 1)
            G.memset(cmask, 0.0).then_inc(s_id, 1)
            pool.wait_ge(s_id, 5)
            G.affine_select(out=ident[:, :], in_=ident[:, :], compare_op=ALU.not_equal, fill=1.0, base=0,
                            pattern=[[-1, P]], channel_multiplier=1).then_inc(s_id, 1)
            G.affine_select(out=cmask, in_=cmask, compare_op=ALU.is_ge, fill=NEG, base=-(CMP_LEN - 1),
                            pattern=[[P, TILES], [-CMP_STRIDE, NCMP]], channel_multiplier=1).then_inc(s_id, 1)
            for i, (n, g, br) in enumerate(BATCH):
                w = NCMP if br == CMP else P * len(key_tiles(n, br))
                pool.wait_ge(s_sc, i + 1)
                for r in range(REP):
                    last = G.tensor_scalar(sw[:, i % 3, r, 0:w], sw[:, i % 3, r, 0:w],
                                           scl[:, i, r:r + 1], None, ALU.mult)
                last.then_inc(s_pp, 1)
            pool.wait_ge(s_oe, 2 * TILES * GROUPS)
            G.iota(iota50, pattern=[[1, NCAND]], base=0, channel_multiplier=0,
                   allow_small_or_imprecise_dtypes=True).then_inc(s_id, 1)

            def stage(col, b):
                G.tensor_copy(slot[b][:, :], eidx[:, bass.ds(col, 1)]).then_inc(s_slot, 1)

            def gather(b):
                G.indirect_dma_start(out=rows[:, b % SLOTS, :], out_offset=None, in_=a["uv"],
                                     in_offset=bass.IndirectOffsetOnAxis(ap=slot[b][:, :], axis=0)
                                     ).then_inc(s_row[b % SLOTS], 16)

            body = 2 * SLOTS

            def refill(col, b):
                pool.wait_ge(s_dot, col - SLOTS + 2)
                pool.wait_ge(s_use, col - SLOTS + 1 + GRP + 1)
                pool.wait_ge(s_slot, col + 1)
                stage(col + 1, (b + 1) % body)
                gather(b)

            pool.wait_ge(s_tk, 1)
            stage(0, 0)
            for b in range(SLOTS):
                pool.wait_ge(s_slot, b + 1)
                stage(b + 1, b + 1)
                gather(b)
            for b in range(SLOTS, body):
                if b + 1 == TK:
                    pool.wait_ge(s_tk, 2)
                refill(b, b)
            for t in range(TILES):
                with pool.Fori(1 if t == 0 else 0, COLS // body - 1) as i:
                    for b in range(body):
                        refill(i * body + (t * COLS + b), b)
                for b in range(body):
                    if t < TILES - 1 and b == body - 1:
                        pool.wait_ge(s_tk, t + 3)
                    refill((t + 1) * COLS - body + b, b)

        @block.scalar
        def _(act):
            nac = [0]

            def after(ins):
                nac[0] += 1
                ins.then_inc(s_ac, 1)
                act.wait_ge(s_ac, nac[0])

            act.wait_ge(s_id, 2)

            def norm_rows(t, col):
                after(A.activation(hn[:, t, :], xs[:, t, :], ACT.Square, accum_out=stat[:, col + t:col + t + 1]))

            for t in range(TILES):
                act.wait_ge(s_xin[t], 16)
                norm_rows(t, 0)
            A.activation(stat[:, 4:8], stat[:, 0:4], ACT.Sqrt, scale=1.0 / D, bias=epsc[:, :]).then_inc(s_ssq, 1)
            act.wait_ge(s_const, 16)
            for k in range(KC):
                act.wait_ge(s_tr, k + 1)
                A.activation(hT[:, k, :], ps[k][:, :], ACT.Copy, scale=gmix[:, k:k + 1]).then_inc(s_hT, 1)
            for j in range(11):
                act.wait_ge(s_z, j + 1)
                q = j < 4 or 5 <= j < 9
                A.activation(qk[:, j, :], ps[j % 8], ACT.Copy, scale=SCALE if q else 1.0).then_inc(s_zo, 1)
            for j in range(4):
                act.wait_ge(s_c1, j + 1)
                A.activation(gT[:, j // 2, j % 2, :], ps[1 + j][:, 0:GROUPS * NCMP], ACT.Gelu_apprx_tanh).then_inc(s_g, 1)
            for t in range(TILES):
                act.wait_ge(s_z, ZT + t + 1)
                A.activation(vn[:, t, :], ps[(ZT + t) % 8][:, 0:NAT_COLS], ACT.Copy).then_inc(s_zo, 1)
            act.wait_ge(s_zo, 11 + TILES)
            for t in range(TILES):
                last = A.activation(gsig[:, t, :], vn[:, t, 384:408], ACT.Sigmoid)
            last.then_inc(s_zo, 1)

            def pt_evac(i):
                n, g, br = BATCH[i]
                rowsn = NCMP if br == CMP else P
                for q in range(PAIRS[i], PAIRS[i + 1]):
                    if q % 2 == 0:
                        act.wait_ge(s_pt, q + 1)
                        if q >= 4:
                            act.wait_ge(s_pv, q - 3)
                        A.activation(pts[0:rowsn, q % 4, :], ps[3 + q % 3][0:rowsn, :], ACT.Copy).then_inc(s_pea, 1)

            for i in range(len(BATCH) + 2):
                if i >= 2:
                    pt_evac(i - 2)
                if i < len(BATCH):
                    n, g, br = BATCH[i]
                    w = NCMP if br == CMP else P * len(key_tiles(n, br))
                    act.wait_ge(s_nm, i + 1)
                    if br == SWA:
                        A.activation(esk[:, i, :], esk[:, i, :], ACT.Exp)
                    for r in range(REP):
                        last = A.activation(sw[:, i % 3, r, 0:w], sw[:, i % 3, r, 0:w], ACT.Exp,
                                            bias=nm[:, i, r:r + 1], accum_out=den[:, i, r:r + 1])
                    last.then_inc(s_ex, 1)
            for m in range(KC):
                for j in range(2):
                    act.wait_ge(s_m, 4 * m + j + 1)
                    if m >= 2:
                        act.wait_ge(s_mT, m - 1)
                    A.activation(sg[:, m % 2, j, :], ps[4 * (m % 2) + j][:, :], ACT.Sigmoid).then_inc(s_sg, 1)
            def peer_norm(t0, t1):
                for t in range(t0, t1):
                    act.wait_ge(s_x1, 2 * t + 2)
                    norm_rows(t, 8)
                A.activation(stat[:, 12 + t0:12 + t1], stat[:, 8 + t0:8 + t1], ACT.Sqrt, scale=1.0 / D,
                             bias=epsc[:, :]).then_inc(s_ssq, 1)

            peer_norm(0, 1)
            for c in range(2):
                act.wait_ge(s_tr, KC + c + 1)
                A.activation(h2T[:, 4 * c:4 * c + 4, 0:P], ps[c].rearrange("p (a b) -> p a b", a=4), ACT.Copy).then_inc(s_hT, 1)
            peer_norm(1, TILES)

            def score_evac(t, c):
                act.wait_ge(s_s, 4 * t + c + 1)
                A.activation(s12[t][:, 4 * c:4 * c + 4, :], ps[4 + c].rearrange("p (a b) -> p a b", a=4),
                             ACT.Copy).then_inc(s_so, 1)

            for c in range(4):
                act.wait_ge(s_q, 4 * c + 4)
                A.activation(qT0[:, 4 * c:4 * c + 4, :], ps[c].rearrange("p (a b) -> p a b", a=4), ACT.Copy).then_inc(s_qo, 1)
                if c:
                    score_evac(0, c - 1)
            score_evac(0, 3)
            for k in range(KC):
                act.wait_ge(s_tr, KC + 2 + k + 1)
                A.activation(h2T[:, k, P:S], ps[k % 4][:, 0:S - P], ACT.Copy).then_inc(s_hT, 1)

            def gate_exp(t):
                act.wait_ge(s_gd, t + 1)
                A.activation(gdif, gdif, ACT.Exp).then_inc(s_ge, 1)

            def tail_norm(t):
                act.wait_ge(s_tx, t + 1)
                A.activation(tsig, xs[:, t, :], ACT.Square, accum_out=stat[:, 16:17]).then_inc(s_t1, 1)
                act.wait_ge(s_t1, 2 * t + 1)
                A.activation(stat[:, 17:18], stat[:, 16:17], ACT.Sqrt, scale=1.0 / D, bias=epsc[:, :]).then_inc(s_t1, 1)

            def tail_gate(t):
                for c in range(2):
                    act.wait_ge(s_t5, 2 * t + c + 1)
                    A.activation(tsig[:, c * HALF:(c + 1) * HALF], ps[6 + c], ACT.Sigmoid).then_inc(s_t6, 1)

            def tail_last_norm(t):
                act.wait_ge(s_t7, t + 1)
                A.activation(tsig, xs[:, t, :], ACT.Square, accum_out=stat[:, 20:21]).then_inc(s_t8, 1)
                act.wait_ge(s_t8, 2 * t + 1)
                A.activation(stat[:, 21:22], stat[:, 20:21], ACT.Sqrt, scale=1.0 / D, bias=epsc[:, :]).then_inc(s_t8, 1)

            def load_rows(t):
                if t:
                    act.wait_ge(s_dot, t * COLS + 1)
                else:
                    act.wait_ge(s_hT, 2 * KC + 2)
                for c in range(2):
                    A.activation(ps[c], hn[:, t, c * HALF:(c + 1) * HALF], ACT.Copy).then_inc(s_hp, 1)

            def query_evac(j):
                act.wait_ge(s_q, 2 * PH + j + 1)
                A.activation(qT1[:, j, :], ps[4 + j % 4][:, 0:S - P], ACT.Copy).then_inc(s_qo, 1)

            load_rows(0)
            for j in range(4):
                query_evac(j)
            gate_exp(0)
            for t in range(TILES):
                if t:
                    load_rows(t)
                for seg in range(SEGS[t]):
                    first, pairs = segment(t, seg)
                    with act.Fori(0, pairs) as i:
                        for e in range(2):
                            q = i * 2 + (first + e)
                            act.wait_ge(s_dot, q * GRP + GRP + 1)
                            A.activation(gel[:, e, :], dots[:, e, :], ACT.Gelu_apprx_tanh).then_inc(s_gel, 1)
                            act.wait_ge(s_wt, q + 1)
                            act.wait_ge(s_use, q * GRP + 1)
                            for b in range(GRP):
                                A.activation(diag[:, e * GRP + b, :], ident[:, :], ACT.Copy,
                                             scale=wts[:, e, b:b + 1]).then_inc(s_dg, 1)
                    if t == 0:
                        if 1 <= seg <= 6:
                            query_evac(2 + 2 * seg)
                            query_evac(3 + 2 * seg)
                        if seg in SCORE_SEGS:
                            for c in range(4):
                                score_evac(SCORE_SEGS.index(seg) + 1, c)
                        if seg == 11:
                            gate_exp(1)
                    elif t < TILES - 1 and seg == 3:
                        gate_exp(t + 1)
                    if t:
                        if seg == 0:
                            tail_norm(t - 1)
                        if seg == 5:
                            tail_gate(t - 1)
                        if seg == 6:
                            tail_last_norm(t - 1)
            tail_norm(TILES - 1)
            tail_gate(TILES - 1)
            tail_last_norm(TILES - 1)

        @block.vector
        def _(dve):
            ndv = [0]

            def after(ins):
                ndv[0] += 1
                ins.then_inc(s_dv, 1)
                dve.wait_ge(s_dv, ndv[0])

            def rows_normed(first, src_col):
                dve.wait_ge(s_ssq, first)
                after(V.reciprocal(stat[:, src_col + 16:src_col + 20], stat[:, src_col:src_col + 4]))

            V.memset(relb[BUCKETS:BUCKETS + 1, :], NEG).then_inc(s_neg, 1)
            dve.wait_ge(s_rb, 1)
            V.tensor_copy(rbias[0:2 * HEADS, 0:HALF], ps[6][0:2 * HEADS, :])
            after(V.tensor_copy(rbias[0:2 * HEADS, HALF:S + P], ps[7][0:2 * HEADS, 0:P]))
            V.memset(rbias[0:HEADS, 2 * P - 1:S + P], NEG).then_inc(s_rbo, 1)
            dve.wait_ge(s_ssq, 1)
            after(V.reciprocal(stat[:, 24:28], stat[:, 4:8]))
            for t in range(TILES):
                V.tensor_scalar(hn[:, t, :], xs[:, t, :], stat[:, 24 + t:25 + t], None, ALU.mult).then_inc(s_xn, 1)
            for kv in range(2):
                j = 11 + kv
                dve.wait_ge(s_z, j + 1)
                for g in range(GROUPS):
                    src = ps[j % 8][g * DH:(g + 1) * DH, :]
                    for par in range(2):
                        v = bass.AP(tensor=src.tensor, offset=src.offset + par,
                                    ap=[list(src.ap[0]), [2, LPAIR], [CMP_STRIDE, NCMP]])
                        pos = posT[g * DH:(g + 1) * DH, par:CMP_LEN:2].unsqueeze(2).broadcast_to([DH, LPAIR, NCMP])
                        V.tensor_tensor(cm[par * DH:(par + 1) * DH, kv, :, g * NCMP:(g + 1) * NCMP], v, pos,
                                        ALU.add).then_inc(s_cm, 1)
            dve.wait_ge(s_c2, 1)
            for g in range(GROUPS):
                V.tensor_copy(kcT[g * DH:(g + 1) * DH, :], ps[3][0:DH, g * NCMP:(g + 1) * NCMP])
                last = V.tensor_copy(vcs[0:NCMP, g, :], ps[4][0:NCMP, g * DH:(g + 1) * DH])
            last.then_inc(s_kc, 1)

            def scores(i):
                n, g, br = BATCH[i]
                if i >= 3:
                    dve.wait_ge(s_pt, PAIRS[i - 2])
                if br == CMP:
                    dve.wait_ge(s_qk, 4 * i + 4)
                    src = ps[(4 * i) % 3][:, 0:REP * NCMP].rearrange("p (r c) -> p r c", r=REP)
                    mask = cmask[:, n, :].unsqueeze(1).broadcast_to([P, REP, NCMP])
                    V.tensor_tensor(sw[:, i % 3, :, 0:NCMP], src, mask, ALU.add).then_inc(s_tt, 4)
                    dve.wait_ge(s_tt, 4 * i + 4)
                    after(V.tensor_reduce(mx[:, i, :], sw[:, i % 3, :, 0:NCMP], AX.X, ALU.max))
                    V.tensor_scalar(nm[:, i, :], mx[:, i, :], NEG / 10, -1.0, ALU.max, ALU.mult).then_inc(s_nm, 1)
                    return
                w = P * len(key_tiles(n, br))
                for r in range(REP):
                    h = g * REP + r
                    bias = (biasA if br == SWA else biasB)[:, h, w - 1::-1]
                    dve.wait_ge(s_qk, 4 * i + r + 1)
                    V.tensor_tensor_reduce(out=sw[:, i % 3, r, 0:w], in0=ps[(4 * i + r) % 3][:, 0:w], in1=bias,
                                           scale=1.0, scalar=sink[:, h:h + 1] if br == SWA else NEG,
                                           op0=ALU.add, op1=ALU.max, accum_out=mx[:, i, r:r + 1]).then_inc(s_tt, 1)
                dve.wait_ge(s_tt, 4 * i + 4)
                ins = V.tensor_scalar(nm[:, i, :], mx[:, i, :], -1.0, None, ALU.mult)
                if br == SWA:
                    after(ins)
                    ins = V.tensor_tensor(esk[:, i, :], sink[:, g * REP:(g + 1) * REP], nm[:, i, :], ALU.add)
                ins.then_inc(s_nm, 1)

            def row_scales(i):
                n, g, br = BATCH[i]
                dve.wait_ge(s_ex, i + 1)
                if br == SWA:
                    after(V.tensor_tensor(den[:, i, :], den[:, i, :], esk[:, i, :], ALU.add))
                after(V.tensor_scalar(den[:, i, :], den[:, i, :], 1e-30, None, ALU.max))
                if br == SWA:
                    V.reciprocal(scl[:, i, :], den[:, i, :]).then_inc(s_sc, 1)
                    return
                after(V.reciprocal(rcp[:, i, :], den[:, i, :]))
                k = {CMP: 0, SLC: 1, WIN: 2}[br]
                V.tensor_tensor(scl[:, i, :], rcp[:, i, :], gsig[:, n, k * HEADS + g * REP:k * HEADS + (g + 1) * REP],
                                ALU.mult).then_inc(s_sc, 1)

            def pt_evac(i):
                n, g, br = BATCH[i]
                rowsn = NCMP if br == CMP else P
                for q in range(PAIRS[i], PAIRS[i + 1]):
                    if q % 2:
                        dve.wait_ge(s_pt, q + 1)
                        if q >= 4:
                            dve.wait_ge(s_pv, q - 3)
                        V.tensor_copy(pts[0:rowsn, q % 4, :], ps[3 + q % 3][0:rowsn, :]).then_inc(s_ped, 1)
                if br in (SWA, CMP):
                    dve.wait_ge(s_pv, PAIRS[i + 1])
                    dst, src = (oTA, ps[6]) if br == SWA else (oTB, ps[7])
                    src = src[0:DH, :].rearrange("p (a b t) -> p a b t", a=2, b=2)
                    for b in range(2):
                        last = V.tensor_copy(dst[b * DH:(b + 1) * DH, 2 * g:2 * g + 2, n * P:(n + 1) * P], src[:, :, b, :])
                    last.then_inc(s_oe, 1)

            dve.wait_ge(s_bias, 16 * 2 * HEADS)
            dve.wait_ge(s_id, 7)
            dve.wait_ge(s_zo, 11 + TILES + 1)
            for i in range(len(BATCH) + 2):
                if i < len(BATCH):
                    scores(i)
                if 1 <= i <= len(BATCH):
                    row_scales(i - 1)
                if i >= 2:
                    pt_evac(i - 2)
            for m in range(KC):
                b = 4 * (m % 2)
                for j in range(2):
                    dve.wait_ge(s_m, 4 * m + 3 + j)
                    dve.wait_ge(s_sg, 2 * m + j + 1)
                    last = V.tensor_tensor(sg[:, m % 2, j, :], sg[:, m % 2, j, :], ps[b + 2 + j][:, :], ALU.mult)
                after(last)
                V.tensor_tensor(mT[:, m, :], sg[:, m % 2, 0, :], sg[:, m % 2, 1, :], ALU.add).then_inc(s_mT, 1)
            def add_mixer(t):
                for c in range(2):
                    dve.wait_ge(s_o, 2 * t + c + 1)
                    V.tensor_tensor(xs[:, t, c * HALF:(c + 1) * HALF], xs[:, t, c * HALF:(c + 1) * HALF],
                                    ps[2 * t + c][:, :], ALU.add).then_inc(s_x1, 1)

            def peer_norm(t0, t1):
                dve.wait_ge(s_ssq, 2 + (t0 > 0))
                after(V.reciprocal(stat[:, 28 + t0:28 + t1], stat[:, 12 + t0:12 + t1]))
                for t in range(t0, t1):
                    V.scalar_tensor_tensor(hn[:, t, :], xs[:, t, :], stat[:, 28 + t:29 + t], gffn[:, :],
                                           ALU.mult, ALU.mult).then_inc(s_xn, 1)

            dve.wait_ge(s_const, 32)
            add_mixer(0)
            add_mixer(1)
            peer_norm(0, 1)
            add_mixer(2)
            add_mixer(3)
            peer_norm(1, TILES)
            dve.wait_ge(s_id, 8)

            def scratch(t):
                return hn[:, t - 1, :] if t else scr_0

            def top_of_halves(t, j0, j1):
                sc = s12[t]
                rest = scratch(t).rearrange("p (j n) -> p j n", n=PK)
                dve.wait_ge(s_so, 4 * t + j1 // 4)
                for j in range(j0, j1):
                    last = V.max(vals[:, j, 0:8], sc[:, j, :])
                after(last)
                for j in range(j0, j1):
                    V.max_index(idxu[:, j, 0:8], vals[:, j, 0:8], sc[:, j, :])
                    last = V.match_replace(rest[:, j - j0, :], vals[:, j, 0:8], sc[:, j, :], -3e38)
                after(last)
                for j in range(j0, j1):
                    last = V.max(vals[:, j, 8:16], rest[:, j - j0, :])
                after(last)
                for j in range(j0, j1):
                    last = V.max_index(idxu[:, j, 8:16], vals[:, j, 8:16], rest[:, j - j0, :])
                after(last)

            def pair_up():
                after(V.tensor_copy(idxf, idxu))
                i4 = idxf.rearrange("p (h s) k -> p h s k", s=2)
                v4 = vals.rearrange("p (h s) k -> p h s k", s=2)
                after(V.tensor_scalar(i4[:, :, 0, :], i4[:, :, 0, :], float(PK), None, ALU.mult))
                for src, dst in ((v4, cand), (i4, cidx)):
                    off = 0
                    for a0, na, nb in RUNS:
                        d = dst[:, :, off:off + na * nb].rearrange("p h (x y) -> p h x y", x=na)
                        last = V.tensor_tensor(d, src[:, :, 0, a0:a0 + na].unsqueeze(3).broadcast_to([P, PH, na, nb]),
                                               src[:, :, 1, 0:nb].unsqueeze(2).broadcast_to([P, PH, na, nb]), ALU.add)
                        off += na * nb
                after(last)

            def top_pairs(t):
                for h in range(PH):
                    last = V.max(tops[:, h, 0:8], cand[:, h, :])
                after(last)
                for h in range(PH):
                    V.max_index(posu[:, h, 0:8], tops[:, h, 0:8], cand[:, h, :])
                    last = V.match_replace(crest[:, h, :], tops[:, h, 0:8], cand[:, h, :], -3e38)
                after(last)
                for h in range(PH):
                    last = V.max(tops[:, h, 8:16], crest[:, h, :])
                after(last)
                for h in range(PH):
                    V.max_index(posu[:, h, 8:16], tops[:, h, 8:16], crest[:, h, :])
                V.tensor_tensor(gdif, tops, tops[:, :, 0:1].broadcast_to([P, PH, TK]), ALU.subtract).then_inc(s_gd, 1)
                dve.wait_ge(s_gd, t + 1)
                after(V.tensor_copy(posf, posu))

            def number_experts(t, h0, h1):
                eq = (scratch(t) if t else junk)[:, 0:TK * NCAND].rearrange("p (k c) -> p k c", k=TK)
                for h in range(h0, h1):
                    after(V.tensor_tensor(eq, iota50.unsqueeze(1).broadcast_to([P, TK, NCAND]),
                                          posf[:, h, :].unsqueeze(2).broadcast_to([P, TK, NCAND]), ALU.is_equal))
                    after(V.tensor_tensor(eq, eq, cidx[:, h, :].unsqueeze(1).broadcast_to([P, TK, NCAND]), ALU.mult))
                    after(V.tensor_reduce(esel[:, h, :], eq, AX.X, ALU.add))

            def publish(t, h0, h1):
                V.tensor_copy(eidx[:, t * COLS + h0 * TK:t * COLS + h1 * TK],
                              esel[:, h0:h1, :].rearrange("p h k -> p (h k)")).then_inc(s_tk, 1)

            def gates(t):
                dve.wait_ge(s_ge, t + 1)
                after(V.tensor_reduce(gsum, gdif, AX.X, ALU.add))
                after(V.reciprocal(grec, gsum))
                after(V.tensor_tensor(gate[:, t * COLS:(t + 1) * COLS].rearrange("p (h k) -> p h k", h=PH),
                                      gdif, grec.unsqueeze(2).broadcast_to([P, PH, TK]), ALU.mult))

            def tail_read(t):
                dve.wait_ge(s_acc, t + 1)
                for c in range(2):
                    last = V.tensor_copy(xs[:, t, c * HALF:(c + 1) * HALF], ps[2 + 2 * (t % 2) + c])
                last.then_inc(s_tx, 1)

            def tail_scale(t):
                dve.wait_ge(s_t1, 2 * t + 2)
                after(V.reciprocal(stat[:, 18:19], stat[:, 17:18]))
                V.tensor_scalar(hn[:, t, :], xs[:, t, :], stat[:, 18:19], None, ALU.mult).then_inc(s_t2, 1)

            def tail_turned(t):
                for c in range(2):
                    dve.wait_ge(s_t3, 2 * t + c + 1)
                    V.tensor_tensor(tT[:, 4 * c:4 * c + 4, :], ps[6 + c].rearrange("p (a b) -> p a b", a=4),
                                    gple[:, 4 * c:4 * c + 4].unsqueeze(2).broadcast_to([P, 4, P]), ALU.mult).then_inc(s_t4, 1)

            def tail_add(t):
                dve.wait_ge(s_t9, t + 1)
                for c in range(2):
                    dve.wait_ge(s_t6, 2 * t + c + 1)
                    last = V.tensor_tensor(tsig[:, c * HALF:(c + 1) * HALF], tsig[:, c * HALF:(c + 1) * HALF],
                                           ps[EMBED[t] + c], ALU.mult)
                after(last)
                V.tensor_tensor(xs[:, t, :], xs[:, t, :], tsig, ALU.add).then_inc(s_t7, 1)

            def tail_out(t):
                dve.wait_ge(s_t8, 2 * t + 2)
                after(V.reciprocal(stat[:, 22:23], stat[:, 21:22]))
                V.scalar_tensor_tensor(xs[:, t, :], xs[:, t, :], stat[:, 22:23], gfin[:, :],
                                       ALU.mult, ALU.mult).then_inc(s_tail, 1)

            for c in range(4):
                top_of_halves(0, 4 * c, 4 * c + 4)
            pair_up()
            top_pairs(0)
            number_experts(0, 0, 1)
            publish(0, 0, 1)
            number_experts(0, 1, PH)
            publish(0, 1, PH)
            gates(0)
            V.memset(dots[:, :, :], 0.0).then_inc(s_dot, 1)
            for t in range(TILES):
                dve.wait_ge(s_hp, 2 * t + 2)
                for seg in range(SEGS[t]):
                    first, pairs = segment(t, seg)
                    with dve.Fori(0, pairs) as i:
                        for e in range(2):
                            q = i * 2 + (first + e)
                            for b in range(GRP):
                                s = e * GRP + b
                                dve.wait_ge(s_dot, q * GRP + (b + 1))
                                dve.wait_ge(s_row[s], i * 16 + (first // 2 + 1) * 16)
                                V.tensor_tensor_reduce(out=junk, in0=hp2, in1=rows[:, s, 0:D],
                                                       scale=1.0, scalar=0.0, op0=ALU.mult, op1=ALU.add,
                                                       accum_out=dots[:, e, b:b + 1]).then_inc(s_dot, 1)
                            dve.wait_ge(s_gel, q + 1)
                            V.tensor_tensor(wts[:, e, :], gel[:, e, :],
                                            gate[:, bass.ds(i * (2 * GRP) + (first + e) * GRP, GRP)],
                                            ALU.mult).then_inc(s_wt, 1)
                    if t < TILES - 1:
                        part = seg if t else seg - 8
                        if part in (0, 1):
                            top_of_halves(t + 1, 8 * part, 8 * part + 8)
                        if part == 2:
                            pair_up()
                        if part == 3:
                            top_pairs(t + 1)
                        if part in (4, 5):
                            number_experts(t + 1, 4 * (part - 4), 4 * (part - 4) + 4)
                        if part == 5:
                            publish(t + 1, 0, PH)
                            gates(t + 1)
                    if t:
                        if seg == 0:
                            tail_read(t - 1)
                        if seg == 1:
                            tail_scale(t - 1)
                        if seg == 2:
                            tail_turned(t - 1)
                        if seg == 6:
                            tail_add(t - 1)
                        if seg == 7:
                            tail_out(t - 1)
            last_tile = TILES - 1
            tail_read(last_tile)
            tail_scale(last_tile)
            tail_turned(last_tile)
            tail_add(last_tile)
            tail_out(last_tile)

        @block.tensor
        def _(pe):
            def arrive(b):
                pe.wait_ge(s_w[b % RING], 16 * (b // RING + 1))

            def blk(b):
                return ring[:, b % RING, :]

            pe.wait_ge(s_rel, 32)
            pe.wait_ge(s_id, 7)
            pe.wait_ge(s_neg, 1)
            T.matmul(ps[6][0:2 * HEADS, :], relb[:, :], hot[:, 0:HALF], start=True, stop=True)
            T.matmul(ps[7][0:2 * HEADS, 0:P], relb[:, :], hot[:, HALF:S + P], start=True, stop=True).then_inc(s_rb, 1)
            pe.wait_ge(s_rbo, 1)

            pe.wait_ge(s_xn, TILES)
            for k in range(KC):
                for t in range(TILES):
                    last = T.transpose(ps[k][:, t * P:(t + 1) * P], hn[:, t, k * P:(k + 1) * P], ident[:, :])
                last.then_inc(s_tr, 1)
            pe.wait_ge(s_hT, KC)
            for j in range(ZT):
                arrive(j)
                if j >= 8:
                    pe.wait_ge(s_zo, j - 7)
                for k in range(KC):
                    last = T.matmul(ps[j % 8], blk(j)[:, k * P:(k + 1) * P], hT[:, k, :],
                                    start=(k == 0), stop=(k == KC - 1))
                last.then_inc(s_z, 1)
            for kv in range(2):
                pe.wait_ge(s_cm, 4 * kv + 4)
                if kv == 0:
                    pe.wait_ge(s_zo, 11)
                for b in range(4):
                    arrive(B_W1 + 4 * kv + b)
                for hb in range(2):
                    for l in range(LPAIR):
                        w = blk(B_W1 + 4 * kv + l // 4)[:, (l % 4) * CMP_HID + hb * P:(l % 4) * CMP_HID + (hb + 1) * P]
                        last = T.matmul(ps[1 + 2 * kv + hb][:, 0:GROUPS * NCMP], w, cm[:, kv, l, :],
                                        start=(l == 0), stop=(l == LPAIR - 1))
                    last.then_inc(s_c1, 1)
            for b in range(NATB):
                arrive(B_NAT + b)
            for t in range(TILES):
                j = ZT + t
                for k in range(KC):
                    w = blk(B_NAT + k // 2)[:, (k % 2) * HALF:(k % 2) * HALF + NAT_COLS]
                    last = T.matmul(ps[j % 8][:, 0:NAT_COLS], hT[:, k, t * P:(t + 1) * P], w,
                                    start=(k == 0), stop=(k == KC - 1))
                last.then_inc(s_z, 1)
            pe.wait_ge(s_g, 4)
            for hb in range(2):
                T.matmul(ps[3][0:DH, 0:GROUPS * NCMP], w2[:, 0, hb, :], gT[:, 0, hb, :], start=(hb == 0), stop=(hb == 1))
            for g in range(GROUPS):
                for hb in range(2):
                    last = T.matmul(ps[4][0:NCMP, g * DH:(g + 1) * DH], gT[:, 1, hb, g * NCMP:(g + 1) * NCMP],
                                    w2[:, 1, hb, :], start=(hb == 0), stop=(hb == 1))
            last.then_inc(s_c2, 1)

            def queries_keys(i):
                n, g, br = BATCH[i]
                half = slice(g * DH, (g + 1) * DH)
                kts = key_tiles(n, br)
                w = P * len(kts)
                for r in range(REP):
                    u = 4 * i + r
                    q = qk[half, r if br == SWA else 5 + r, n * P:(n + 1) * P]
                    if u >= 3 and (br != CMP or r == 0):
                        pe.wait_ge(s_tt, u - 2)
                    if br == CMP:
                        T.matmul(ps[(4 * i) % 3][:, r * NCMP:(r + 1) * NCMP], q, kcT[half, :],
                                 start=True, stop=True).then_inc(s_qk, 1)
                    else:
                        k = qk[half, {SWA: 4, SLC: 9, WIN: 10}[br], kts[0] * P:kts[0] * P + w]
                        T.matmul(ps[u % 3][:, 0:w], q, k, start=True, stop=True).then_inc(s_qk, 1)

            def weigh_values(i):
                n, g, br = BATCH[i]
                kts = key_tiles(n, br)
                keys = NCMP if br == CMP else P
                pe.wait_ge(s_pp, i + 1)

                def turn(x):
                    q = PAIRS[i] + x
                    if q >= 3:
                        ev, od = evac_counts(q - 3)
                        pe.wait_ge(s_pea, ev) if (q - 3) % 2 == 0 else pe.wait_ge(s_ped, od)
                    for r in range(REP):
                        last = T.transpose(ps[3 + q % 3][0:keys, r * P:(r + 1) * P],
                                           sw[:, i % 3, r, x * P:x * P + keys], ident[:, :])
                    last.then_inc(s_pt, 1)

                def apply(x):
                    q = PAIRS[i] + x
                    ev, od = evac_counts(q)
                    pe.wait_ge(s_pea, ev) if q % 2 == 0 else pe.wait_ge(s_ped, od)
                    if br == CMP:
                        val = vcs[0:NCMP, g, :]
                    else:
                        c = {SWA: 0, SLC: 128, WIN: 256}[br] + g * DH
                        val = vn[:, kts[x], c:c + DH]
                    T.matmul(ps[6 if br == SWA else 7][0:DH, :], val, pts[0:keys, q % 4, :],
                             start=(x == 0 and br in (SWA, SLC)),
                             stop=(x == len(kts) - 1 and br in (SWA, CMP))).then_inc(s_pv, 1)

                og = 2 * (n * GROUPS + g)
                turn(0)
                if br in (SWA, SLC) and og:
                    pe.wait_ge(s_oe, og - 1 if br == SWA else og)
                for x in range(1, len(kts)):
                    turn(x)
                    apply(x - 1)
                apply(len(kts) - 1)

            pe.wait_ge(s_kc, 1)
            pe.wait_ge(s_zo, 11 + TILES)
            for i in range(len(BATCH) + 2):
                if i < len(BATCH):
                    queries_keys(i)
                if i >= 2:
                    weigh_values(i - 2)
            pe.wait_ge(s_oe, 2 * TILES * GROUPS)
            for m in range(KC):
                base = 4 * (m % 2)
                for j in range(2):
                    b = B_MG + 3 * m + j
                    arrive(b)
                    if m >= 2:
                        pe.wait_ge(s_mT, m - 1)
                    for k in range(KC):
                        last = T.matmul(ps[base + j], blk(b)[:, k * P:(k + 1) * P], hT[:, k, :],
                                        start=(k == 0), stop=(k == KC - 1))
                    last.then_inc(s_m, 1)
                b = B_MG + 3 * m + 2
                arrive(b)
                for j, oT in enumerate((oTA, oTB)):
                    for c in range(4):
                        last = T.matmul(ps[base + 2 + j], blk(b)[:, (4 * j + c) * P:(4 * j + c + 1) * P], oT[:, c, :],
                                        start=(c == 0), stop=(c == 3))
                    last.then_inc(s_m, 1)
            for k in range(KC):
                arrive(B_WO + k)
                if k == 0:
                    pe.wait_ge(s_mT, KC)
                for t in range(TILES):
                    for c in range(2):
                        last = T.matmul(ps[2 * t + c], mT[:, k, t * P:(t + 1) * P],
                                        blk(B_WO + k)[:, c * HALF:(c + 1) * HALF], start=(k == 0), stop=(k == KC - 1))
                        if k == KC - 1:
                            last.then_inc(s_o, 1)
                if k < KC - 1:
                    last.then_inc(s_wo, 1)
            pe.wait_ge(s_xn, TILES + 1)
            for c in range(2):
                for k in range(4):
                    last = T.transpose(ps[c][:, k * P:(k + 1) * P], hn[:, 0, (4 * c + k) * P:(4 * c + k + 1) * P],
                                       ident[:, :])
                last.then_inc(s_tr, 1)

            def scores(t, c):
                for j in range(4 * c, 4 * c + 4):
                    q = qT0[:, j, :] if t == 0 else qT1[:, j, (t - 1) * P:t * P]
                    last = T.matmul(ps[4 + c][:, (j % 4) * PK:(j % 4 + 1) * PK], q,
                                    pkeys[:, j % 2, :], start=True, stop=True)
                last.then_inc(s_s, 1)

            pe.wait_ge(s_hT, KC + 2)
            for c in range(4):
                for j in range(4 * c, 4 * c + 4):
                    arrive(B_WQ + j)
                    for k in range(KC):
                        last = T.matmul(ps[c][:, (j % 4) * P:(j % 4 + 1) * P], blk(B_WQ + j)[:, k * P:(k + 1) * P],
                                        h2T[:, k, 0:P], start=(k == 0), stop=(k == KC - 1))
                    last.then_inc(s_q, 1)
                if c == 1:
                    pe.wait_ge(s_x1, 2 * TILES)
                if c:
                    pe.wait_ge(s_qo, c)
                    scores(0, c - 1)
            pe.wait_ge(s_qo, 4)
            scores(0, 3)
            pe.wait_ge(s_xn, 2 * TILES)
            for k in range(KC):
                if k >= 4:
                    pe.wait_ge(s_hT, KC + 2 + k - 3)
                for t in range(1, TILES):
                    last = T.transpose(ps[k % 4][:, (t - 1) * P:t * P], hn[:, t, k * P:(k + 1) * P], ident[:, :])
                last.then_inc(s_tr, 1)

            def other_queries(j):
                arrive(B_WQ2 + j)
                if j >= 4:
                    pe.wait_ge(s_qo, 4 + j - 3)
                for k in range(KC):
                    last = T.matmul(ps[4 + j % 4][:, 0:S - P], blk(B_WQ2 + j)[:, k * P:(k + 1) * P],
                                    h2T[:, k, P:S], start=(k == 0), stop=(k == KC - 1))
                last.then_inc(s_q, 1)

            pe.wait_ge(s_hT, 2 * KC + 2)
            pe.wait_ge(s_so, 4)
            for j in range(4):
                other_queries(j)

            def open_sum(t):
                if t >= 2:
                    pe.wait_ge(s_tx, t - 1)
                for c in range(2):
                    last = T.matmul(ps[2 + 2 * (t % 2) + c], ident[:, :], xs[:, t, c * HALF:(c + 1) * HALF],
                                    start=True, stop=False)
                return last

            def tail_turn(t):
                pe.wait_ge(s_t2, t + 1)
                if t:
                    pe.wait_ge(s_t7, t)
                for c in range(2):
                    for k in range(4):
                        last = T.transpose(ps[6 + c][:, k * P:(k + 1) * P], hn[:, t, (4 * c + k) * P:(4 * c + k + 1) * P],
                                           ident[:, :])
                    last.then_inc(s_t3, 1)

            def tail_gate(t, c):
                pe.wait_ge(s_const, 16 * 6)
                pe.wait_ge(s_t4, 2 * t + 2)
                for k in range(KC):
                    last = T.matmul(ps[6 + c], tT[:, k, :], wpg[:, k, c * HALF:(c + 1) * HALF],
                                    start=(k == 0), stop=(k == KC - 1))
                last.then_inc(s_t5, 1)

            def tail_embed(t):
                if t < TILES - 1:
                    pe.wait_ge(s_t6, 2 * t + 2)
                else:
                    pe.wait_ge(s_tx, t)
                for c in range(2):
                    for k in range(2):
                        last = T.matmul(ps[EMBED[t] + c], pT[:, k, t * P:(t + 1) * P], wple[:, k, c * HALF:(c + 1) * HALF],
                                        start=(k == 0), stop=(k == 1))
                last.then_inc(s_t9, 1)

            for t in range(TILES):
                if t == 1:
                    pe.wait_ge(s_so, 4 * TILES)
                if t == 0:
                    open_sum(0).then_inc(s_use, GRP + 1)
                else:
                    open_sum(t)
                for seg in range(SEGS[t]):
                    first, pairs = segment(t, seg)
                    with pe.Fori(0, pairs) as i:
                        for s in range(SLOTS):
                            pe.wait_ge(s_dg, i * SLOTS + (first * GRP + s + 1))
                            for c in range(2):
                                last = T.matmul(ps[2 + 2 * (t % 2) + c], diag[:, s, :],
                                                rows[:, s, D + c * HALF:D + (c + 1) * HALF], start=False, stop=False)
                            last.then_inc(s_use, 1)
                    if t == 0:
                        if seg < 6:
                            other_queries(4 + 2 * seg)
                            other_queries(5 + 2 * seg)
                        if seg in SCORE_SEGS:
                            later = SCORE_SEGS.index(seg) + 1
                            if later == 1:
                                pe.wait_ge(s_qo, 4 + 2 * PH)
                            pe.wait_ge(s_so, 4 * later)
                            for c in range(4):
                                scores(later, c)
                    if t:
                        if seg == 1:
                            tail_turn(t - 1)
                        if seg in (3, 4):
                            tail_gate(t - 1, seg - 3)
                        if seg == 5:
                            tail_embed(t - 1)
                        if seg == 6 and t == TILES - 1:
                            tail_embed(t)
                for c in range(2):
                    last = T.matmul(ps[2 + 2 * (t % 2) + c], zero[:, :], xs[:, t, c * HALF:(c + 1) * HALF],
                                    start=False, stop=True)
                last.then_inc(s_acc, 1)
            tail_turn(TILES - 1)
            for c in range(2):
                tail_gate(TILES - 1, c)


OUT_SHAPE = (1, S, D)


def lay_out(i):
    f = {k: np.asarray(v) for k, v in i.items()}
    w_in = f["w_in"][0]
    ar = np.arange

    def by_chunk(w, cols):
        return w[:, cols].reshape(KC, P, len(cols)).transpose(1, 0, 2).reshape(P, -1)

    q_a, k_a, v_a, q_b = 0, 512, 640, 768
    k_c, v_c, k_s, v_s, k_w, v_w, b_g, m_g = 1280, 1408, 1536, 1664, 1792, 1920, 2048, 2072
    pair = lambda base, r: np.concatenate([ar(DH) + base + r * DH, ar(DH) + base + (r + REP) * DH])
    run = lambda base: ar(P) + base
    zcols = [pair(q_a, r) for r in range(REP)] + [run(k_a)] + [pair(q_b, r) for r in range(REP)]
    zcols += [run(k_s), run(k_w), run(k_c), run(v_c)]
    blocks = [by_chunk(w_in, c) for c in zcols]
    nat = np.concatenate([run(v_a), run(v_s), run(v_w), ar(3 * HEADS) + b_g])
    wn = np.zeros((P, KC, HALF), np.float32)
    wn[:, :, :NAT_COLS] = by_chunk(w_in, nat).reshape(P, KC, NAT_COLS)
    for w in ("cmp_k_w1", "cmp_v_w1"):
        w1 = f[w][0].reshape(LPAIR, P, CMP_HID)
        blocks += [w1[4 * b:4 * b + 4].transpose(1, 0, 2).reshape(P, D) for b in range(4)]
    blocks += [wn[:, 2 * b:2 * b + 2].reshape(P, D) for b in range(NATB)]
    for m in range(KC):
        blocks += [by_chunk(w_in, run(m_g + m * P)), by_chunk(w_in, run(m_g + D + m * P))]
        up = np.concatenate([f["w_up_a"][0], f["w_up_b"][0]])
        blocks.append(by_chunk(up, run(m * P)))
    blocks += [f["w_o"][0][k * P:(k + 1) * P] for k in range(KC)]
    blocks += [by_chunk(f["peer_wq"][0], run(j * P)) for j in range(2 * PH)]
    pos = f["cmp_pos"][0].T
    w2 = np.stack([f["cmp_k_w2"][0].reshape(2, P, DH), f["cmp_v_w2"][0].reshape(2, P, DH)])
    small = np.concatenate([
        f["g_mix"][0].reshape(KC, P).T, f["g_ple"][0].reshape(KC, P).T, np.concatenate([pos, pos]),
        np.broadcast_to(f["a_sink"][0].reshape(1, HEADS), (P, HEADS)),
        w2.transpose(2, 0, 1, 3).reshape(P, -1),
        f["peer_k1"][0].T, f["peer_k2"][0].T], axis=1)
    rel = f["rel_bias"]
    return {
        "x": f["x"][0],
        "small": small,
        "rel_bias": rel,
        "hot": bucket_onehot(),
        "wpack": np.stack(blocks),
        "g_ffn": np.broadcast_to(f["g_ffn"][0][None], (P, D)),
        "g_final": np.broadcast_to(f["g_final"][None], (P, D)),
        "pT": f["p"][0, 0].T.reshape(2, P, S).transpose(1, 0, 2),
        "w_ple": f["w_ple"][0].reshape(2, P, D).transpose(1, 0, 2),
        "w_pg": f["w_ple_gate"][0].reshape(KC, P, D).transpose(1, 0, 2),
        "uv": np.concatenate([f["peer_u"][0], f["peer_v"][0]], axis=1),
    }


def kernel(**inputs):
    import concourse.bacc as bacc
    from concourse.bass_utils import run_bass_kernel_spmd

    nc = bacc.Bacc("TRN2", target_bir_lowering=False, num_devices=1)
    arrays, aps = {}, {}
    for name, v in lay_out(inputs).items():
        v = np.ascontiguousarray(v)
        arrays[f"in_{name}"] = v
        aps[name] = nc.dram_tensor(f"in_{name}", v.shape, mybir.dt.from_np(v.dtype), kind="ExternalInput").ap()
    out = nc.dram_tensor("out", (S, D), mybir.dt.float32, kind="ExternalOutput").ap()
    build(nc, aps, out)
    got = run_bass_kernel_spmd(nc, [arrays], core_ids=[0])
    return got.results[0]["out"].reshape(OUT_SHAPE)
```

```python
import math
from contextlib import ExitStack

import numpy as np

import concourse.bass as bass
from concourse import mybir

D = 1024
S = 512
P = 128
TILES = S // P
KC = D // P
HALF = 512
DH = 64
HEADS = 8
GROUPS = 2
REP = HEADS // GROUPS
BUCKETS, MAX_EXACT, MAX_DIST = 32, 16, 128
CMP_LEN, CMP_STRIDE, CMP_HID = 32, 16, 256
NCMP = S // CMP_STRIDE - CMP_LEN // CMP_STRIDE + 1
LPAIR = CMP_LEN // 2
PK = 128
PH = 8
TK = 16
COLS = PH * TK
PLE = 256
EPS = 1e-6
NEG = -1e30
SCALE = DH ** -0.5

RUNS = [(0, 1, 16), (1, 1, 8), (2, 1, 5), (3, 1, 4), (4, 1, 3), (5, 3, 2), (8, 8, 1)]
NCAND = sum(na * nb for _, na, nb in RUNS)

ZT = 13
NAT_COLS = 3 * 128 + 24
NATB = 4
B_W1 = ZT
B_NAT = B_W1 + 8
B_MG = B_NAT + NATB
B_WO = B_MG + 3 * KC
B_WQ = B_WO + KC
B_WO2 = B_WQ + 2 * PH
B_WQ2 = B_WO2 + KC
NBLK = B_WQ2 + 2 * PH
RING = 6

SLOTS = 8
GRP = 4
GROUPS_T = COLS // GRP
SEGS = (16, 8, 8, 8)
assert SLOTS == 2 * GRP and all(GROUPS_T % (2 * n) == 0 for n in SEGS)


def bucket_onehot():
    width = S + P
    out = np.zeros((BUCKETS + 1, width), np.float32)
    for y in range(width):
        dist = y - (P - 1)
        if dist < 0:
            out[BUCKETS, y] = 1.0
            continue
        b = dist
        if dist >= MAX_EXACT:
            b = MAX_EXACT + int(math.log(dist / MAX_EXACT) / math.log(MAX_DIST / MAX_EXACT) * (BUCKETS - MAX_EXACT))
            b = min(b, BUCKETS - 1)
        out[b, y] = 1.0
    return out


def build(nc, a, out):
    f32, i32, u32 = mybir.dt.float32, mybir.dt.int32, mybir.dt.uint32
    ALU, ACT, AX = mybir.AluOpType, mybir.ActivationFunctionType, mybir.AxisListType
    V, T, A, G = nc.vector, nc.tensor, nc.scalar, nc.gpsimd
    ctx = ExitStack()
    with ctx:
        def sb(name, shape, dt=f32):
            return ctx.enter_context(nc.sbuf_tensor(name, shape, dt))

        def sem(name):
            return ctx.enter_context(nc.semaphore(name))

        xs = sb("xs", [P, TILES, D])
        hn = sb("hn", [P, TILES, D])
        ring = sb("ring", [P, RING, D])
        ident = sb("ident", [P, P])
        zero = sb("zero", [P, P])
        small = sb("small", [P, 8 + 8 + CMP_LEN + 8 + 256 + 256])
        gmix, gple = small[:, 0:8], small[:, 8:16]
        posT = small[:, 16:48]
        sink = small[:, 48:56]
        w2 = small[:, 56:312].rearrange("p (v h d) -> p v h d", v=2, h=2)
        pkeys = small[:, 312:568].rearrange("p (h n) -> p h n", h=2)
        eidx = sb("eidx", [P, TILES * COLS + 1], i32)
        gate = sb("gate", [P, TILES * COLS])
        stat = sb("stat", [P, 64])
        ARENA = 34420
        ar = sb("arena", [P, ARENA])

        def place(start, shape, dt=None):
            n = int(np.prod(shape))
            assert start + n <= ARENA, (start, shape)
            v = ar[:, start:start + n]
            if dt is not None:
                v = v.bitcast(dt)
            if len(shape) == 2:
                v = v.rearrange("p (a b) -> p a b", a=shape[0])
            if len(shape) == 3:
                v = v.rearrange("p (a b c) -> p a b c", a=shape[0], b=shape[1])
            return v, start + n

        at = 0
        hT, at = place(at, [KC, S])
        at_q = at
        qk, at = place(at, [11, S])
        vn, at = place(at, [TILES, NAT_COLS])
        gsig, at = place(at, [TILES, 24])
        biasB, at = place(at, [HEADS, S])
        biasA, at = place(at, [HEADS, 2 * P])
        sw, at = place(at, [3, REP, S])
        pts, at = place(at, [4, S])
        cm, at = place(at, [2, LPAIR, GROUPS * NCMP])
        gT, at = place(at, [2, 2, GROUPS * NCMP])
        kcT, at = place(at, [NCMP])
        vcs, at = place(at, [GROUPS, DH])
        cmask, at = place(at, [TILES, NCMP])
        oTA, at = place(at, [4, S])
        oTB, at = place(at, [4, S])
        mx, at = place(at, [32, REP])
        nm, at = place(at, [32, REP])
        den, at = place(at, [32, REP])
        rcp, at = place(at, [32, REP])
        scl, at = place(at, [32, REP])
        esk, at = place(at, [32, REP])
        rbias, _ = place(at_q + 11 * S + TILES * NAT_COLS + TILES * 24 + 6 * S * 2, [S + P])
        sg, _ = place(at_q + 11 * S + TILES * NAT_COLS + TILES * 24, [2, 2, S])
        s12_0, ra = place(at_q, [2 * PH, PK])
        scr_0, ra = place(ra, [D])
        assert ra <= SLOTS * 2 * D
        ringf = ring.rearrange("p a b -> p (a b)")
        s12 = [s12_0] + [ringf[:, i * 2 * PH * PK:(i + 1) * 2 * PH * PK].rearrange("p (j n) -> p j n", j=2 * PH)
                         for i in range(TILES - 1)]
        rows, pa = place(0, [SLOTS, 2 * D])
        junk, pa = place(pa, [D])
        diag, pa = place(pa, [2 * GRP, P])
        late = pa
        wpg, pa = place(pa, [KC, D])
        tT, pa = place(pa, [KC, P])
        tsig, pa = place(pa, [D])
        wple, pa = place(pa, [2, D])
        pT, pa = place(pa, [2, S])
        h2T, qa = place(late, [KC, S])
        mT, _ = place(qa, [KC, S])
        qT1, qa = place(qa, [2 * PH, S - P])
        qT0, qa = place(qa, [2 * PH, P])
        assert qa <= pa
        vals, pa = place(pa, [2 * PH, TK])
        idxu, pa = place(pa, [2 * PH, TK], u32)
        idxf, pa = place(pa, [2 * PH, TK])
        cand, pa = place(pa, [PH, NCAND])
        crest, pa = place(pa, [PH, NCAND])
        cidx, pa = place(pa, [PH, NCAND])
        tops, pa = place(pa, [PH, TK])
        posu, pa = place(pa, [PH, TK], u32)
        posf, pa = place(pa, [PH, TK])
        esel, pa = place(pa, [PH, TK])
        gdif, pa = place(pa, [PH, TK])
        iota50, pa = place(pa, [NCAND])
        gsum, pa = place(pa, [PH])
        grec, pa = place(pa, [PH])
        gffn = sb("gffn", [P, D])
        gfin = gffn
        slot = [sb(f"slot{b}", [P, 1], i32) for b in range(2 * SLOTS)]
        dots = sb("dots", [P, 2, GRP])
        gel = sb("gel", [P, 2, GRP])
        wts = sb("wts", [P, 2, GRP])
        relb = sb("relb", [BUCKETS + 1, 2 * HEADS])
        hot, _ = place(0, [S + P])
        hot = hot[0:BUCKETS + 1, :]
        epsc = sb("epsc", [P, 1])

        psum = ctx.enter_context(nc.psum_tensor("psum", [P, 8, HALF], f32))
        ps = [psum[:, i, :] for i in range(8)]
        hp2 = psum[:, 0:2, :].rearrange("p a b -> p (a b)")
        rdram = nc.dram_tensor("bias_rows", (2 * HEADS, S + P), f32, kind="Internal").ap()

        x_loaded = [sem(f"x_loaded{t}") for t in range(TILES)]
        consts_loaded = sem("consts_loaded")
        rel_loaded = sem("rel_loaded")
        mask_row_set = sem("mask_row_set")
        block_loaded = [sem(f"block_loaded{i}") for i in range(RING)]
        wo_block_used = sem("wo_block_used")
        pool_consts_set = sem("pool_consts_set")
        rms_ready = sem("rms_ready")
        rows_normed = sem("rows_normed")
        rows_turned = sem("rows_turned")
        hT_ready = sem("hT_ready")
        proj_ready = sem("proj_ready")
        proj_out = sem("proj_out")
        windows_ready = sem("windows_ready")
        bias_rows_ready = sem("bias_rows_ready")
        bias_rows_out = sem("bias_rows_out")
        bias_rows_stored = sem("bias_rows_stored")
        bias_tiles_loaded = sem("bias_tiles_loaded")
        cmp_hidden_ready = sem("cmp_hidden_ready")
        cmp_gelu_ready = sem("cmp_gelu_ready")
        cmp_made = sem("cmp_made")
        cmp_out = sem("cmp_out")
        scores_ready = sem("scores_ready")
        scores_biased = sem("scores_biased")
        max_ready = sem("max_ready")
        exp_ready = sem("exp_ready")
        dve_step = sem("dve_step")
        act_step = sem("act_step")
        scale_ready = sem("scale_ready")
        probs_ready = sem("probs_ready")
        probs_turned = sem("probs_turned")
        turned_out_act = sem("turned_out_act")
        turned_out_dve = sem("turned_out_dve")
        values_added = sem("values_added")
        heads_out = sem("heads_out")
        merge_ready = sem("merge_ready")
        merge_gate_ready = sem("merge_gate_ready")
        merged = sem("merged")
        wo_ready = sem("wo_ready")
        wo_added = sem("wo_added")
        query_ready = sem("query_ready")
        query_out = sem("query_out")
        keyscores_ready = sem("keyscores_ready")
        keyscores_out = sem("keyscores_out")
        gate_args_ready = sem("gate_args_ready")
        gate_exps_ready = sem("gate_exps_ready")
        experts_known = sem("experts_known")
        index_staged = sem("index_staged")
        row_gathered = [sem(f"row_gathered{b}") for b in range(SLOTS)]
        dot_ready = sem("dot_ready")
        gelu_ready = sem("gelu_ready")
        weights_ready = sem("weights_ready")
        diag_ready = sem("diag_ready")
        column_used = sem("column_used")
        dot_rows_ready = sem("dot_rows_ready")
        sum_ready = sem("sum_ready")
        sum_out = sem("sum_out")
        tail_rms = sem("tail_rms")
        tail_rrms = sem("tail_rrms")
        tail_turned_pe = sem("tail_turned_pe")
        tail_lhs_ready = sem("tail_lhs_ready")
        tail_gate_made = sem("tail_gate_made")
        tail_gate_ready = sem("tail_gate_ready")
        tail_added = sem("tail_added")
        final_rms = sem("final_rms")
        tail_embed_made = sem("tail_embed_made")
        tile_done = sem("tile_done")
        out_stored = sem("out_stored")

        BATCH = [(n, g, br) for n in range(TILES) for g in range(GROUPS) for br in range(4)]
        SWA, SLC, WIN, CMP = range(4)

        def key_tiles(n, br):
            if br == SWA:
                return [n - 1, n] if n else [0]
            if br == CMP:
                return [0]
            return list(range(n + 1))

        PAIRS = [0]
        for n_, g_, br_ in BATCH:
            PAIRS.append(PAIRS[-1] + len(key_tiles(n_, br_)))

        def evac_counts(q):
            return q // 2 + 1, (q + 1) // 2

        def segment(t, seg):
            groups = GROUPS_T // SEGS[t]
            return t * GROUPS_T + seg * groups, groups // 2

        def used_up(b):
            if b < ZT:
                return proj_ready, b + 1
            if b < B_NAT:
                return cmp_hidden_ready, 2 * ((b - B_W1) // 4) + 2
            if b < B_MG:
                return proj_ready, ZT + TILES
            if b < B_WO:
                m, j = divmod(b - B_MG, 3)
                return merge_ready, 4 * m + (1, 2, 4)[j]
            if b < B_WQ:
                return (wo_block_used, b - B_WO + 1) if b < B_WQ - 1 else (wo_ready, 2)
            if b < B_WO2:
                return query_ready, b - B_WQ + 1
            if b < B_WQ2:
                return (wo_block_used, KC + b - B_WO2) if b < B_WQ2 - 1 else (wo_ready, 2 * TILES)
            return query_ready, 2 * PH + b - B_WQ2 + 1

        EMBED = (6, 6, 6, 2)
        SCORE_SEGS = (9, 11, 13)

        block = ctx.enter_context(nc.Block())

        @block.sync
        def _(sp):
            for t in range(TILES):
                sp.dma_start(xs[:, t, :], a["x"][t * P:(t + 1) * P, :]).then_inc(x_loaded[t], 16)
            sp.dma_start(small[:, :], a["small"]).then_inc(consts_loaded, 16)
            sp.dma_start(relb[0:BUCKETS, :], a["rel_bias"]).then_inc(rel_loaded, 16)
            sp.dma_start(hot[:, :], a["hot"]).then_inc(rel_loaded, 16)

            for b in range(NBLK):
                if b >= RING:
                    sp.wait_ge(*used_up(b - RING))
                src = b if b < B_WO2 else b - (B_WO2 - B_WO if b < B_WQ2 else B_WQ2 - B_WQ)
                sp.dma_start(ring[:, b % RING, :], a["wpack"][src, :, :]).then_inc(block_loaded[b % RING], 16)
                if b == 0:
                    sp.wait_ge(bias_rows_out, 1)
                    sp.dma_start(rdram, rbias[0:2 * HEADS, :]).then_inc(bias_rows_stored, 16)
                    sp.wait_ge(bias_rows_stored, 16)
                    for h in range(2 * HEADS):
                        w = 2 * P if h < HEADS else S
                        dst = biasA[:, h, :] if h < HEADS else biasB[:, h - HEADS, :]
                        src = bass.AP(tensor=rdram.tensor, offset=h * (S + P), ap=[[1, P], [1, w]])
                        sp.dma_start(dst, src).then_inc(bias_tiles_loaded, 16)
                    sp.dma_start(gffn[:, :], a["g_ffn"]).then_inc(consts_loaded, 16)
            sp.wait_ge(keyscores_ready, 4 * TILES)
            sp.dma_start(wpg, a["w_pg"]).then_inc(consts_loaded, 16)
            sp.dma_start(wple, a["w_ple"]).then_inc(consts_loaded, 16)
            sp.dma_start(pT, a["pT"]).then_inc(consts_loaded, 16)
            sp.dma_start(gfin[:, :], a["g_final"]).then_inc(consts_loaded, 16)
            for t in range(TILES):
                sp.wait_ge(tile_done, t + 1)
                sp.dma_start(out[t * P:(t + 1) * P, :], xs[:, t, :]).then_inc(out_stored, 16)
            sp.wait_ge(out_stored, 16 * TILES)

        @block.gpsimd
        def _(pool):
            G.memset(zero[:, :], 0.0).then_inc(pool_consts_set, 1)
            G.memset(epsc[:, :], EPS).then_inc(pool_consts_set, 1)
            G.memset(eidx[:, TILES * COLS:], 0).then_inc(pool_consts_set, 1)
            G.memset(ident[:, :], 0.0).then_inc(pool_consts_set, 1)
            G.memset(cmask, 0.0).then_inc(pool_consts_set, 1)
            pool.wait_ge(pool_consts_set, 5)
            G.affine_select(out=ident[:, :], in_=ident[:, :], compare_op=ALU.not_equal, fill=1.0, base=0,
                            pattern=[[-1, P]], channel_multiplier=1).then_inc(pool_consts_set, 1)
            G.affine_select(out=cmask, in_=cmask, compare_op=ALU.is_ge, fill=NEG, base=-(CMP_LEN - 1),
                            pattern=[[P, TILES], [-CMP_STRIDE, NCMP]], channel_multiplier=1).then_inc(pool_consts_set, 1)
            for i, (n, g, br) in enumerate(BATCH):
                w = NCMP if br == CMP else P * len(key_tiles(n, br))
                pool.wait_ge(scale_ready, i + 1)
                for r in range(REP):
                    last = G.tensor_scalar(sw[:, i % 3, r, 0:w], sw[:, i % 3, r, 0:w],
                                           scl[:, i, r:r + 1], None, ALU.mult)
                last.then_inc(probs_ready, 1)
            pool.wait_ge(heads_out, 2 * TILES * GROUPS)
            G.iota(iota50, pattern=[[1, NCAND]], base=0, channel_multiplier=0,
                   allow_small_or_imprecise_dtypes=True).then_inc(pool_consts_set, 1)

            def stage(col, b):
                G.tensor_copy(slot[b][:, :], eidx[:, bass.ds(col, 1)]).then_inc(index_staged, 1)

            def gather(b):
                G.indirect_dma_start(out=rows[:, b % SLOTS, :], out_offset=None, in_=a["uv"],
                                     in_offset=bass.IndirectOffsetOnAxis(ap=slot[b][:, :], axis=0)
                                     ).then_inc(row_gathered[b % SLOTS], 16)

            body = 2 * SLOTS

            def refill(col, b):
                pool.wait_ge(dot_ready, col - SLOTS + 2)
                pool.wait_ge(column_used, col - SLOTS + 1 + GRP + 1)
                pool.wait_ge(index_staged, col + 1)
                stage(col + 1, (b + 1) % body)
                gather(b)

            pool.wait_ge(experts_known, 1)
            stage(0, 0)
            for b in range(SLOTS):
                pool.wait_ge(index_staged, b + 1)
                stage(b + 1, b + 1)
                gather(b)
            for b in range(SLOTS, body):
                if b + 1 == TK:
                    pool.wait_ge(experts_known, 2)
                refill(b, b)
            for t in range(TILES):
                with pool.Fori(1 if t == 0 else 0, COLS // body - 1) as i:
                    for b in range(body):
                        refill(i * body + (t * COLS + b), b)
                for b in range(body):
                    if t < TILES - 1 and b == body - 1:
                        pool.wait_ge(experts_known, t + 3)
                    refill((t + 1) * COLS - body + b, b)

        @block.scalar
        def _(act):
            nac = [0]

            def after(ins):
                nac[0] += 1
                ins.then_inc(act_step, 1)
                act.wait_ge(act_step, nac[0])

            act.wait_ge(pool_consts_set, 2)

            def norm_rows(t, col):
                after(A.activation(hn[:, t, :], xs[:, t, :], ACT.Square, accum_out=stat[:, col + t:col + t + 1]))

            for t in range(TILES):
                act.wait_ge(x_loaded[t], 16)
                norm_rows(t, 0)
            A.activation(stat[:, 4:8], stat[:, 0:4], ACT.Sqrt, scale=1.0 / D, bias=epsc[:, :]).then_inc(rms_ready, 1)
            act.wait_ge(consts_loaded, 16)
            for k in range(KC):
                act.wait_ge(rows_turned, k + 1)
                A.activation(hT[:, k, :], ps[k][:, :], ACT.Copy, scale=gmix[:, k:k + 1]).then_inc(hT_ready, 1)
            for j in range(11):
                act.wait_ge(proj_ready, j + 1)
                q = j < 4 or 5 <= j < 9
                A.activation(qk[:, j, :], ps[j % 8], ACT.Copy, scale=SCALE if q else 1.0).then_inc(proj_out, 1)
            for j in range(4):
                act.wait_ge(cmp_hidden_ready, j + 1)
                A.activation(gT[:, j // 2, j % 2, :], ps[1 + j][:, 0:GROUPS * NCMP], ACT.Gelu_apprx_tanh).then_inc(cmp_gelu_ready, 1)
            for t in range(TILES):
                act.wait_ge(proj_ready, ZT + t + 1)
                A.activation(vn[:, t, :], ps[(ZT + t) % 8][:, 0:NAT_COLS], ACT.Copy).then_inc(proj_out, 1)
            act.wait_ge(proj_out, 11 + TILES)
            for t in range(TILES):
                last = A.activation(gsig[:, t, :], vn[:, t, 384:408], ACT.Sigmoid)
            last.then_inc(proj_out, 1)

            def pt_evac(i):
                n, g, br = BATCH[i]
                rowsn = NCMP if br == CMP else P
                for q in range(PAIRS[i], PAIRS[i + 1]):
                    if q % 2 == 0:
                        act.wait_ge(probs_turned, q + 1)
                        if q >= 4:
                            act.wait_ge(values_added, q - 3)
                        A.activation(pts[0:rowsn, q % 4, :], ps[3 + q % 3][0:rowsn, :], ACT.Copy).then_inc(turned_out_act, 1)

            for i in range(len(BATCH) + 2):
                if i >= 2:
                    pt_evac(i - 2)
                if i < len(BATCH):
                    n, g, br = BATCH[i]
                    w = NCMP if br == CMP else P * len(key_tiles(n, br))
                    act.wait_ge(max_ready, i + 1)
                    if br == SWA:
                        A.activation(esk[:, i, :], esk[:, i, :], ACT.Exp)
                    for r in range(REP):
                        last = A.activation(sw[:, i % 3, r, 0:w], sw[:, i % 3, r, 0:w], ACT.Exp,
                                            bias=nm[:, i, r:r + 1], accum_out=den[:, i, r:r + 1])
                    last.then_inc(exp_ready, 1)
            for m in range(KC):
                for j in range(2):
                    act.wait_ge(merge_ready, 4 * m + j + 1)
                    if m >= 2:
                        act.wait_ge(merged, m - 1)
                    A.activation(sg[:, m % 2, j, :], ps[4 * (m % 2) + j][:, :], ACT.Sigmoid).then_inc(merge_gate_ready, 1)
            def peer_norm(t0, t1):
                for t in range(t0, t1):
                    act.wait_ge(wo_added, 2 * t + 2)
                    norm_rows(t, 8)
                A.activation(stat[:, 12 + t0:12 + t1], stat[:, 8 + t0:8 + t1], ACT.Sqrt, scale=1.0 / D,
                             bias=epsc[:, :]).then_inc(rms_ready, 1)

            peer_norm(0, 1)
            for c in range(2):
                act.wait_ge(rows_turned, KC + c + 1)
                A.activation(h2T[:, 4 * c:4 * c + 4, 0:P], ps[c].rearrange("p (a b) -> p a b", a=4), ACT.Copy).then_inc(hT_ready, 1)

            def score_evac(t, c):
                act.wait_ge(keyscores_ready, 4 * t + c + 1)
                A.activation(s12[t][:, 4 * c:4 * c + 4, :], ps[4 + c].rearrange("p (a b) -> p a b", a=4),
                             ACT.Copy).then_inc(keyscores_out, 1)

            for c in range(4):
                act.wait_ge(query_ready, 4 * c + 4)
                A.activation(qT0[:, 4 * c:4 * c + 4, :], ps[c].rearrange("p (a b) -> p a b", a=4), ACT.Copy).then_inc(query_out, 1)
                if c:
                    score_evac(0, c - 1)
            score_evac(0, 3)
            def gate_exp(t):
                act.wait_ge(gate_args_ready, t + 1)
                A.activation(gdif, gdif, ACT.Exp).then_inc(gate_exps_ready, 1)

            def tail_norm(t):
                act.wait_ge(sum_out, t + 1)
                A.activation(tsig, xs[:, t, :], ACT.Square, accum_out=stat[:, 16:17]).then_inc(tail_rms, 1)
                act.wait_ge(tail_rms, 2 * t + 1)
                A.activation(stat[:, 17:18], stat[:, 16:17], ACT.Sqrt, scale=1.0 / D, bias=epsc[:, :]).then_inc(tail_rms, 1)

            def tail_gate(t):
                act.wait_ge(tail_rrms, t + 1)
                for c in range(2):
                    act.wait_ge(tail_gate_made, 2 * t + c + 1)
                    A.activation(tsig[:, c * HALF:(c + 1) * HALF], ps[6 + c], ACT.Sigmoid, scale=stat[:, 18:19]).then_inc(tail_gate_ready, 1)

            def tail_last_norm(t):
                act.wait_ge(tail_added, t + 1)
                A.activation(tsig, xs[:, t, :], ACT.Square, accum_out=stat[:, 20:21]).then_inc(final_rms, 1)
                act.wait_ge(final_rms, 2 * t + 1)
                A.activation(stat[:, 21:22], stat[:, 20:21], ACT.Sqrt, scale=1.0 / D, bias=epsc[:, :]).then_inc(final_rms, 1)

            def query_evac(j):
                act.wait_ge(query_ready, 2 * PH + j + 1)
                A.activation(qT1[:, j, :], ps[4 + j % 4][:, 0:S - P], ACT.Copy).then_inc(query_out, 1)

            gate_exp(0)
            peer_norm(1, TILES)
            for t in range(TILES):
                for seg in range(SEGS[t]):
                    first, pairs = segment(t, seg)
                    with act.Fori(0, pairs) as i:
                        for e in range(2):
                            q = i * 2 + (first + e)
                            act.wait_ge(dot_ready, q * GRP + GRP + 1)
                            A.activation(gel[:, e, :], dots[:, e, :], ACT.Gelu_apprx_tanh).then_inc(gelu_ready, 1)
                            act.wait_ge(weights_ready, q + 1)
                            act.wait_ge(column_used, q * GRP + 1)
                            for b in range(GRP):
                                A.activation(diag[:, e * GRP + b, :], ident[:, :], ACT.Copy,
                                             scale=wts[:, e, b:b + 1]).then_inc(diag_ready, 1)
                    if t == 0:
                        if seg == 0:
                            for k in range(KC):
                                act.wait_ge(rows_turned, KC + 2 + k + 1)
                                A.activation(h2T[:, k, P:S], ps[4 + k % 4][:, 0:S - P], ACT.Copy).then_inc(hT_ready, 1)
                        if 2 <= seg <= 9:
                            query_evac(2 * seg - 4)
                            query_evac(2 * seg - 3)
                        if seg in SCORE_SEGS:
                            for c in range(4):
                                score_evac(SCORE_SEGS.index(seg) + 1, c)
                        if seg == 12:
                            gate_exp(1)
                    elif t < TILES - 1 and seg == 3:
                        gate_exp(t + 1)
                    if t:
                        if seg == 0:
                            tail_norm(t - 1)
                        if seg == 5:
                            tail_gate(t - 1)
                        if seg == 6:
                            tail_last_norm(t - 1)
            tail_norm(TILES - 1)
            tail_gate(TILES - 1)
            tail_last_norm(TILES - 1)

        @block.vector
        def _(dve):
            ndv = [0]

            def after(ins):
                ndv[0] += 1
                ins.then_inc(dve_step, 1)
                dve.wait_ge(dve_step, ndv[0])

            V.memset(relb[BUCKETS:BUCKETS + 1, :], NEG).then_inc(mask_row_set, 1)
            dve.wait_ge(bias_rows_ready, 1)
            V.tensor_copy(rbias[0:2 * HEADS, 0:HALF], ps[6][0:2 * HEADS, :])
            after(V.tensor_copy(rbias[0:2 * HEADS, HALF:S + P], ps[7][0:2 * HEADS, 0:P]))
            V.memset(rbias[0:HEADS, 2 * P - 1:S + P], NEG).then_inc(bias_rows_out, 1)
            dve.wait_ge(rms_ready, 1)
            after(V.reciprocal(stat[:, 24:28], stat[:, 4:8]))
            for t in range(TILES):
                V.tensor_scalar(hn[:, t, :], xs[:, t, :], stat[:, 24 + t:25 + t], None, ALU.mult).then_inc(rows_normed, 1)
            for kv in range(2):
                j = 11 + kv
                dve.wait_ge(proj_ready, j + 1)
                for g in range(GROUPS):
                    src = ps[j % 8][g * DH:(g + 1) * DH, :]
                    for par in range(2):
                        v = bass.AP(tensor=src.tensor, offset=src.offset + par,
                                    ap=[list(src.ap[0]), [2, LPAIR], [CMP_STRIDE, NCMP]])
                        pos = posT[g * DH:(g + 1) * DH, par:CMP_LEN:2].unsqueeze(2).broadcast_to([DH, LPAIR, NCMP])
                        V.tensor_tensor(cm[par * DH:(par + 1) * DH, kv, :, g * NCMP:(g + 1) * NCMP], v, pos,
                                        ALU.add).then_inc(windows_ready, 1)
            dve.wait_ge(cmp_made, 1)
            for g in range(GROUPS):
                V.tensor_copy(kcT[g * DH:(g + 1) * DH, :], ps[3][0:DH, g * NCMP:(g + 1) * NCMP])
                last = V.tensor_copy(vcs[0:NCMP, g, :], ps[4][0:NCMP, g * DH:(g + 1) * DH])
            last.then_inc(cmp_out, 1)

            def scores(i):
                n, g, br = BATCH[i]
                if i >= 3:
                    dve.wait_ge(probs_turned, PAIRS[i - 2])
                if br == CMP:
                    dve.wait_ge(scores_ready, 4 * i + 4)
                    src = ps[(4 * i) % 3][:, 0:REP * NCMP].rearrange("p (r c) -> p r c", r=REP)
                    mask = cmask[:, n, :].unsqueeze(1).broadcast_to([P, REP, NCMP])
                    V.tensor_tensor(sw[:, i % 3, :, 0:NCMP], src, mask, ALU.add).then_inc(scores_biased, 4)
                    dve.wait_ge(scores_biased, 4 * i + 4)
                    after(V.tensor_reduce(mx[:, i, :], sw[:, i % 3, :, 0:NCMP], AX.X, ALU.max))
                    V.tensor_scalar(nm[:, i, :], mx[:, i, :], NEG / 10, -1.0, ALU.max, ALU.mult).then_inc(max_ready, 1)
                    return
                w = P * len(key_tiles(n, br))
                for r in range(REP):
                    h = g * REP + r
                    bias = (biasA if br == SWA else biasB)[:, h, w - 1::-1]
                    dve.wait_ge(scores_ready, 4 * i + r + 1)
                    V.tensor_tensor_reduce(out=sw[:, i % 3, r, 0:w], in0=ps[(4 * i + r) % 3][:, 0:w], in1=bias,
                                           scale=1.0, scalar=sink[:, h:h + 1] if br == SWA else NEG,
                                           op0=ALU.add, op1=ALU.max, accum_out=mx[:, i, r:r + 1]).then_inc(scores_biased, 1)
                dve.wait_ge(scores_biased, 4 * i + 4)
                ins = V.tensor_scalar(nm[:, i, :], mx[:, i, :], -1.0, None, ALU.mult)
                if br == SWA:
                    after(ins)
                    ins = V.tensor_tensor(esk[:, i, :], sink[:, g * REP:(g + 1) * REP], nm[:, i, :], ALU.add)
                ins.then_inc(max_ready, 1)

            def row_scales(i):
                n, g, br = BATCH[i]
                dve.wait_ge(exp_ready, i + 1)
                if br == SWA:
                    after(V.tensor_tensor(den[:, i, :], den[:, i, :], esk[:, i, :], ALU.add))
                after(V.tensor_scalar(den[:, i, :], den[:, i, :], 1e-30, None, ALU.max))
                if br == SWA:
                    V.reciprocal(scl[:, i, :], den[:, i, :]).then_inc(scale_ready, 1)
                    return
                after(V.reciprocal(rcp[:, i, :], den[:, i, :]))
                k = {CMP: 0, SLC: 1, WIN: 2}[br]
                V.tensor_tensor(scl[:, i, :], rcp[:, i, :], gsig[:, n, k * HEADS + g * REP:k * HEADS + (g + 1) * REP],
                                ALU.mult).then_inc(scale_ready, 1)

            def pt_evac(i):
                n, g, br = BATCH[i]
                rowsn = NCMP if br == CMP else P
                for q in range(PAIRS[i], PAIRS[i + 1]):
                    if q % 2:
                        dve.wait_ge(probs_turned, q + 1)
                        if q >= 4:
                            dve.wait_ge(values_added, q - 3)
                        V.tensor_copy(pts[0:rowsn, q % 4, :], ps[3 + q % 3][0:rowsn, :]).then_inc(turned_out_dve, 1)
                if br in (SWA, CMP):
                    dve.wait_ge(values_added, PAIRS[i + 1])
                    dst, src = (oTA, ps[6]) if br == SWA else (oTB, ps[7])
                    src = src[0:DH, :].rearrange("p (a b t) -> p a b t", a=2, b=2)
                    for b in range(2):
                        last = V.tensor_copy(dst[b * DH:(b + 1) * DH, 2 * g:2 * g + 2, n * P:(n + 1) * P], src[:, :, b, :])
                    last.then_inc(heads_out, 1)

            dve.wait_ge(bias_tiles_loaded, 16 * 2 * HEADS)
            dve.wait_ge(pool_consts_set, 7)
            dve.wait_ge(proj_out, 11 + TILES + 1)
            for i in range(len(BATCH) + 2):
                if i < len(BATCH):
                    scores(i)
                if 1 <= i <= len(BATCH):
                    row_scales(i - 1)
                if i >= 2:
                    pt_evac(i - 2)
            for m in range(KC):
                b = 4 * (m % 2)
                for j in range(2):
                    dve.wait_ge(merge_ready, 4 * m + 3 + j)
                    dve.wait_ge(merge_gate_ready, 2 * m + j + 1)
                    last = V.tensor_tensor(sg[:, m % 2, j, :], sg[:, m % 2, j, :], ps[b + 2 + j][:, :], ALU.mult)
                after(last)
                V.tensor_tensor(mT[:, m, :], sg[:, m % 2, 0, :], sg[:, m % 2, 1, :], ALU.add).then_inc(merged, 1)
            def add_mixer(t):
                for c in range(2):
                    dve.wait_ge(wo_ready, 2 * t + c + 1)
                    V.tensor_tensor(xs[:, t, c * HALF:(c + 1) * HALF], xs[:, t, c * HALF:(c + 1) * HALF],
                                    ps[2 * t + c][:, :], ALU.add).then_inc(wo_added, 1)

            def peer_norm(t0, t1):
                dve.wait_ge(rms_ready, 2 + (t0 > 0))
                after(V.reciprocal(stat[:, 28 + t0:28 + t1], stat[:, 12 + t0:12 + t1]))
                for t in range(t0, t1):
                    V.scalar_tensor_tensor(hn[:, t, :], xs[:, t, :], stat[:, 28 + t:29 + t], gffn[:, :],
                                           ALU.mult, ALU.mult).then_inc(rows_normed, 1)

            dve.wait_ge(consts_loaded, 32)
            add_mixer(0)
            peer_norm(0, 1)
            dve.wait_ge(pool_consts_set, 8)

            def scratch(t):
                return hn[:, t - 1, :] if t else scr_0

            def top_of_halves(t, j0, j1):
                sc = s12[t]
                rest = scratch(t).rearrange("p (j n) -> p j n", n=PK)
                dve.wait_ge(keyscores_out, 4 * t + j1 // 4)
                for j in range(j0, j1):
                    last = V.max(vals[:, j, 0:8], sc[:, j, :])
                after(last)
                for j in range(j0, j1):
                    V.max_index(idxu[:, j, 0:8], vals[:, j, 0:8], sc[:, j, :])
                    last = V.match_replace(rest[:, j - j0, :], vals[:, j, 0:8], sc[:, j, :], -3e38)
                after(last)
                for j in range(j0, j1):
                    last = V.max(vals[:, j, 8:16], rest[:, j - j0, :])
                after(last)
                for j in range(j0, j1):
                    last = V.max_index(idxu[:, j, 8:16], vals[:, j, 8:16], rest[:, j - j0, :])
                after(last)

            def pair_up():
                after(V.tensor_copy(idxf, idxu))
                i4 = idxf.rearrange("p (h s) k -> p h s k", s=2)
                v4 = vals.rearrange("p (h s) k -> p h s k", s=2)
                after(V.tensor_scalar(i4[:, :, 0, :], i4[:, :, 0, :], float(PK), None, ALU.mult))
                for src, dst in ((v4, cand), (i4, cidx)):
                    off = 0
                    for a0, na, nb in RUNS:
                        d = dst[:, :, off:off + na * nb].rearrange("p h (x y) -> p h x y", x=na)
                        last = V.tensor_tensor(d, src[:, :, 0, a0:a0 + na].unsqueeze(3).broadcast_to([P, PH, na, nb]),
                                               src[:, :, 1, 0:nb].unsqueeze(2).broadcast_to([P, PH, na, nb]), ALU.add)
                        off += na * nb
                after(last)

            def top_pairs(t):
                for h in range(PH):
                    last = V.max(tops[:, h, 0:8], cand[:, h, :])
                after(last)
                for h in range(PH):
                    V.max_index(posu[:, h, 0:8], tops[:, h, 0:8], cand[:, h, :])
                    last = V.match_replace(crest[:, h, :], tops[:, h, 0:8], cand[:, h, :], -3e38)
                after(last)
                for h in range(PH):
                    last = V.max(tops[:, h, 8:16], crest[:, h, :])
                after(last)
                for h in range(PH):
                    V.max_index(posu[:, h, 8:16], tops[:, h, 8:16], crest[:, h, :])
                V.tensor_tensor(gdif, tops, tops[:, :, 0:1].broadcast_to([P, PH, TK]), ALU.subtract).then_inc(gate_args_ready, 1)
                dve.wait_ge(gate_args_ready, t + 1)
                after(V.tensor_copy(posf, posu))

            def number_experts(t, h0, h1):
                eq = (scratch(t) if t else junk)[:, 0:TK * NCAND].rearrange("p (k c) -> p k c", k=TK)
                for h in range(h0, h1):
                    after(V.tensor_tensor(eq, iota50.unsqueeze(1).broadcast_to([P, TK, NCAND]),
                                          posf[:, h, :].unsqueeze(2).broadcast_to([P, TK, NCAND]), ALU.is_equal))
                    after(V.tensor_tensor(eq, eq, cidx[:, h, :].unsqueeze(1).broadcast_to([P, TK, NCAND]), ALU.mult))
                    after(V.tensor_reduce(esel[:, h, :], eq, AX.X, ALU.add))

            def publish(t, h0, h1):
                V.tensor_copy(eidx[:, t * COLS + h0 * TK:t * COLS + h1 * TK],
                              esel[:, h0:h1, :].rearrange("p h k -> p (h k)")).then_inc(experts_known, 1)

            def gates(t):
                dve.wait_ge(gate_exps_ready, t + 1)
                after(V.tensor_reduce(gsum, gdif, AX.X, ALU.add))
                after(V.reciprocal(grec, gsum))
                after(V.tensor_tensor(gate[:, t * COLS:(t + 1) * COLS].rearrange("p (h k) -> p h k", h=PH),
                                      gdif, grec.unsqueeze(2).broadcast_to([P, PH, TK]), ALU.mult))

            def tail_read(t):
                dve.wait_ge(sum_ready, t + 1)
                for c in range(2):
                    last = V.tensor_copy(xs[:, t, c * HALF:(c + 1) * HALF], ps[2 + 2 * (t % 2) + c])
                last.then_inc(sum_out, 1)

            def tail_scale(t):
                dve.wait_ge(tail_rms, 2 * t + 2)
                V.reciprocal(stat[:, 18:19], stat[:, 17:18]).then_inc(tail_rrms, 1)

            def tail_turned(t):
                for c in range(2):
                    dve.wait_ge(tail_turned_pe, 2 * t + c + 1)
                    V.tensor_tensor(tT[:, 4 * c:4 * c + 4, :], ps[6 + c].rearrange("p (a b) -> p a b", a=4),
                                    gple[:, 4 * c:4 * c + 4].unsqueeze(2).broadcast_to([P, 4, P]), ALU.mult).then_inc(tail_lhs_ready, 1)

            def tail_add(t):
                dve.wait_ge(tail_embed_made, t + 1)
                for c in range(2):
                    dve.wait_ge(tail_gate_ready, 2 * t + c + 1)
                    last = V.tensor_tensor(tsig[:, c * HALF:(c + 1) * HALF], tsig[:, c * HALF:(c + 1) * HALF],
                                           ps[EMBED[t] + c], ALU.mult)
                after(last)
                V.tensor_tensor(xs[:, t, :], xs[:, t, :], tsig, ALU.add).then_inc(tail_added, 1)

            def tail_out(t):
                dve.wait_ge(final_rms, 2 * t + 2)
                after(V.reciprocal(stat[:, 22:23], stat[:, 21:22]))
                V.scalar_tensor_tensor(xs[:, t, :], xs[:, t, :], stat[:, 22:23], gfin[:, :],
                                       ALU.mult, ALU.mult).then_inc(tile_done, 1)

            for c in range(4):
                top_of_halves(0, 4 * c, 4 * c + 4)
            pair_up()
            top_pairs(0)
            number_experts(0, 0, 1)
            publish(0, 0, 1)
            number_experts(0, 1, PH)
            publish(0, 1, PH)
            gates(0)
            V.memset(dots[:, :, :], 0.0).then_inc(dot_ready, 1)
            for t in range(TILES):
                if t == 0:
                    dve.wait_ge(query_out, 2)
                else:
                    dve.wait_ge(dot_ready, t * COLS + 1)
                V.tensor_copy(hp2, hn[:, t, :]).then_inc(dot_rows_ready, 1)
                dve.wait_ge(dot_rows_ready, t + 1)
                if t == 0:
                    for later in range(1, TILES):
                        add_mixer(later)
                for seg in range(SEGS[t]):
                    first, pairs = segment(t, seg)
                    with dve.Fori(0, pairs) as i:
                        for e in range(2):
                            q = i * 2 + (first + e)
                            for b in range(GRP):
                                s = e * GRP + b
                                dve.wait_ge(dot_ready, q * GRP + (b + 1))
                                dve.wait_ge(row_gathered[s], i * 16 + (first // 2 + 1) * 16)
                                V.tensor_tensor_reduce(out=junk, in0=hp2, in1=rows[:, s, 0:D],
                                                       scale=1.0, scalar=0.0, op0=ALU.mult, op1=ALU.add,
                                                       accum_out=dots[:, e, b:b + 1]).then_inc(dot_ready, 1)
                            dve.wait_ge(gelu_ready, q + 1)
                            V.tensor_tensor(wts[:, e, :], gel[:, e, :],
                                            gate[:, bass.ds(i * (2 * GRP) + (first + e) * GRP, GRP)],
                                            ALU.mult).then_inc(weights_ready, 1)
                    if t == 0 and seg == 0:
                        peer_norm(1, TILES)
                    if t < TILES - 1:
                        first_half, second_half, pairing, best = (10, 11, 12, 12) if t == 0 else (0, 1, 2, 3)
                        if seg == first_half:
                            top_of_halves(t + 1, 0, PH)
                        if seg == second_half:
                            top_of_halves(t + 1, PH, 2 * PH)
                        if seg == pairing:
                            pair_up()
                        if seg == best:
                            top_pairs(t + 1)
                        heads = ({13: (0, 4), 14: (4, 8)} if t == 0 else {4: (0, 3), 5: (3, 6), 6: (6, 8)}).get(seg)
                        if heads:
                            number_experts(t + 1, *heads)
                            if heads[1] == PH:
                                publish(t + 1, 0, PH)
                                gates(t + 1)
                    if t:
                        if seg == 0:
                            tail_read(t - 1)
                        if seg == 1:
                            tail_scale(t - 1)
                        if seg == 2:
                            tail_turned(t - 1)
                        if seg == 6:
                            tail_add(t - 1)
                        if seg == 7:
                            tail_out(t - 1)
            last_tile = TILES - 1
            tail_read(last_tile)
            tail_scale(last_tile)
            tail_turned(last_tile)
            tail_add(last_tile)
            tail_out(last_tile)

        @block.tensor
        def _(pe):
            def arrive(b):
                pe.wait_ge(block_loaded[b % RING], 16 * (b // RING + 1))

            def blk(b):
                return ring[:, b % RING, :]

            pe.wait_ge(rel_loaded, 32)
            pe.wait_ge(pool_consts_set, 7)
            pe.wait_ge(mask_row_set, 1)
            T.matmul(ps[6][0:2 * HEADS, :], relb[:, :], hot[:, 0:HALF], start=True, stop=True)
            T.matmul(ps[7][0:2 * HEADS, 0:P], relb[:, :], hot[:, HALF:S + P], start=True, stop=True).then_inc(bias_rows_ready, 1)
            pe.wait_ge(bias_rows_out, 1)

            pe.wait_ge(rows_normed, TILES)
            for k in range(KC):
                for t in range(TILES):
                    last = T.transpose(ps[k][:, t * P:(t + 1) * P], hn[:, t, k * P:(k + 1) * P], ident[:, :])
                last.then_inc(rows_turned, 1)
            pe.wait_ge(hT_ready, KC)
            for j in range(ZT):
                arrive(j)
                if j >= 8:
                    pe.wait_ge(proj_out, j - 7)
                for k in range(KC):
                    last = T.matmul(ps[j % 8], blk(j)[:, k * P:(k + 1) * P], hT[:, k, :],
                                    start=(k == 0), stop=(k == KC - 1))
                last.then_inc(proj_ready, 1)
            for kv in range(2):
                pe.wait_ge(windows_ready, 4 * kv + 4)
                if kv == 0:
                    pe.wait_ge(proj_out, 11)
                for b in range(4):
                    arrive(B_W1 + 4 * kv + b)
                for hb in range(2):
                    for l in range(LPAIR):
                        w = blk(B_W1 + 4 * kv + l // 4)[:, (l % 4) * CMP_HID + hb * P:(l % 4) * CMP_HID + (hb + 1) * P]
                        last = T.matmul(ps[1 + 2 * kv + hb][:, 0:GROUPS * NCMP], w, cm[:, kv, l, :],
                                        start=(l == 0), stop=(l == LPAIR - 1))
                    last.then_inc(cmp_hidden_ready, 1)
            for b in range(NATB):
                arrive(B_NAT + b)
            for t in range(TILES):
                j = ZT + t
                for k in range(KC):
                    w = blk(B_NAT + k // 2)[:, (k % 2) * HALF:(k % 2) * HALF + NAT_COLS]
                    last = T.matmul(ps[j % 8][:, 0:NAT_COLS], hT[:, k, t * P:(t + 1) * P], w,
                                    start=(k == 0), stop=(k == KC - 1))
                last.then_inc(proj_ready, 1)
            pe.wait_ge(cmp_gelu_ready, 4)
            for hb in range(2):
                T.matmul(ps[3][0:DH, 0:GROUPS * NCMP], w2[:, 0, hb, :], gT[:, 0, hb, :], start=(hb == 0), stop=(hb == 1))
            for g in range(GROUPS):
                for hb in range(2):
                    last = T.matmul(ps[4][0:NCMP, g * DH:(g + 1) * DH], gT[:, 1, hb, g * NCMP:(g + 1) * NCMP],
                                    w2[:, 1, hb, :], start=(hb == 0), stop=(hb == 1))
            last.then_inc(cmp_made, 1)

            def queries_keys(i):
                n, g, br = BATCH[i]
                half = slice(g * DH, (g + 1) * DH)
                kts = key_tiles(n, br)
                w = P * len(kts)
                for r in range(REP):
                    u = 4 * i + r
                    q = qk[half, r if br == SWA else 5 + r, n * P:(n + 1) * P]
                    if u >= 3 and (br != CMP or r == 0):
                        pe.wait_ge(scores_biased, u - 2)
                    if br == CMP:
                        T.matmul(ps[(4 * i) % 3][:, r * NCMP:(r + 1) * NCMP], q, kcT[half, :],
                                 start=True, stop=True).then_inc(scores_ready, 1)
                    else:
                        k = qk[half, {SWA: 4, SLC: 9, WIN: 10}[br], kts[0] * P:kts[0] * P + w]
                        T.matmul(ps[u % 3][:, 0:w], q, k, start=True, stop=True).then_inc(scores_ready, 1)

            def weigh_values(i):
                n, g, br = BATCH[i]
                kts = key_tiles(n, br)
                keys = NCMP if br == CMP else P
                pe.wait_ge(probs_ready, i + 1)

                def turn(x):
                    q = PAIRS[i] + x
                    if q >= 3:
                        ev, od = evac_counts(q - 3)
                        pe.wait_ge(turned_out_act, ev) if (q - 3) % 2 == 0 else pe.wait_ge(turned_out_dve, od)
                    for r in range(REP):
                        last = T.transpose(ps[3 + q % 3][0:keys, r * P:(r + 1) * P],
                                           sw[:, i % 3, r, x * P:x * P + keys], ident[:, :])
                    last.then_inc(probs_turned, 1)

                def apply(x):
                    q = PAIRS[i] + x
                    ev, od = evac_counts(q)
                    pe.wait_ge(turned_out_act, ev) if q % 2 == 0 else pe.wait_ge(turned_out_dve, od)
                    if br == CMP:
                        val = vcs[0:NCMP, g, :]
                    else:
                        c = {SWA: 0, SLC: 128, WIN: 256}[br] + g * DH
                        val = vn[:, kts[x], c:c + DH]
                    T.matmul(ps[6 if br == SWA else 7][0:DH, :], val, pts[0:keys, q % 4, :],
                             start=(x == 0 and br in (SWA, SLC)),
                             stop=(x == len(kts) - 1 and br in (SWA, CMP))).then_inc(values_added, 1)

                og = 2 * (n * GROUPS + g)
                turn(0)
                if br in (SWA, SLC) and og:
                    pe.wait_ge(heads_out, og - 1 if br == SWA else og)
                for x in range(1, len(kts)):
                    turn(x)
                    apply(x - 1)
                apply(len(kts) - 1)

            pe.wait_ge(cmp_out, 1)
            pe.wait_ge(proj_out, 11 + TILES)
            for i in range(len(BATCH) + 2):
                if i < len(BATCH):
                    queries_keys(i)
                if i >= 2:
                    weigh_values(i - 2)
            pe.wait_ge(heads_out, 2 * TILES * GROUPS)
            for m in range(KC):
                base = 4 * (m % 2)
                for j in range(2):
                    b = B_MG + 3 * m + j
                    arrive(b)
                    if m >= 2:
                        pe.wait_ge(merged, m - 1)
                    for k in range(KC):
                        last = T.matmul(ps[base + j], blk(b)[:, k * P:(k + 1) * P], hT[:, k, :],
                                        start=(k == 0), stop=(k == KC - 1))
                    last.then_inc(merge_ready, 1)
                b = B_MG + 3 * m + 2
                arrive(b)
                for j, oT in enumerate((oTA, oTB)):
                    for c in range(4):
                        last = T.matmul(ps[base + 2 + j], blk(b)[:, (4 * j + c) * P:(4 * j + c + 1) * P], oT[:, c, :],
                                        start=(c == 0), stop=(c == 3))
                    last.then_inc(merge_ready, 1)
            def project_out(b0, t0, t1):
                for k in range(KC):
                    arrive(b0 + k)
                    for t in range(t0, t1):
                        for c in range(2):
                            last = T.matmul(ps[2 * t + c], mT[:, k, t * P:(t + 1) * P],
                                            blk(b0 + k)[:, c * HALF:(c + 1) * HALF], start=(k == 0), stop=(k == KC - 1))
                            if k == KC - 1:
                                last.then_inc(wo_ready, 1)
                    if k < KC - 1:
                        last.then_inc(wo_block_used, 1)

            pe.wait_ge(merged, KC)
            project_out(B_WO, 0, 1)
            pe.wait_ge(rows_normed, TILES + 1)
            for c in range(2):
                for k in range(4):
                    last = T.transpose(ps[c][:, k * P:(k + 1) * P], hn[:, 0, (4 * c + k) * P:(4 * c + k + 1) * P],
                                       ident[:, :])
                last.then_inc(rows_turned, 1)

            def scores(t, c):
                for j in range(4 * c, 4 * c + 4):
                    q = qT0[:, j, :] if t == 0 else qT1[:, j, (t - 1) * P:t * P]
                    last = T.matmul(ps[4 + c][:, (j % 4) * PK:(j % 4 + 1) * PK], q,
                                    pkeys[:, j % 2, :], start=True, stop=True)
                last.then_inc(keyscores_ready, 1)

            pe.wait_ge(hT_ready, KC + 2)
            for c in range(4):
                for j in range(4 * c, 4 * c + 4):
                    arrive(B_WQ + j)
                    for k in range(KC):
                        last = T.matmul(ps[c][:, (j % 4) * P:(j % 4 + 1) * P], blk(B_WQ + j)[:, k * P:(k + 1) * P],
                                        h2T[:, k, 0:P], start=(k == 0), stop=(k == KC - 1))
                    last.then_inc(query_ready, 1)
                if c:
                    pe.wait_ge(query_out, c)
                    scores(0, c - 1)
            pe.wait_ge(query_out, 4)
            scores(0, 3)
            pe.wait_ge(keyscores_out, 4)
            project_out(B_WO2, 1, TILES)

            def turn_others():
                pe.wait_ge(rows_normed, 2 * TILES)
                for k in range(KC):
                    if k >= 4:
                        pe.wait_ge(hT_ready, KC + 2 + k - 3)
                    for t in range(1, TILES):
                        last = T.transpose(ps[4 + k % 4][:, (t - 1) * P:t * P], hn[:, t, k * P:(k + 1) * P], ident[:, :])
                    last.then_inc(rows_turned, 1)

            def other_queries(j):
                arrive(B_WQ2 + j)
                if j >= 4:
                    pe.wait_ge(query_out, 4 + j - 3)
                for k in range(KC):
                    last = T.matmul(ps[4 + j % 4][:, 0:S - P], blk(B_WQ2 + j)[:, k * P:(k + 1) * P],
                                    h2T[:, k, P:S], start=(k == 0), stop=(k == KC - 1))
                last.then_inc(query_ready, 1)

            def open_sum(t):
                if t >= 2:
                    pe.wait_ge(sum_out, t - 1)
                for c in range(2):
                    last = T.matmul(ps[2 + 2 * (t % 2) + c], ident[:, :], xs[:, t, c * HALF:(c + 1) * HALF],
                                    start=True, stop=False)
                return last

            def tail_turn(t):
                pe.wait_ge(sum_out, t + 1)
                if t:
                    pe.wait_ge(tail_added, t)
                for c in range(2):
                    for k in range(4):
                        last = T.transpose(ps[6 + c][:, k * P:(k + 1) * P], xs[:, t, (4 * c + k) * P:(4 * c + k + 1) * P],
                                           ident[:, :])
                    last.then_inc(tail_turned_pe, 1)

            def tail_gate(t, c):
                pe.wait_ge(consts_loaded, 16 * 6)
                pe.wait_ge(tail_lhs_ready, 2 * t + 2)
                for k in range(KC):
                    last = T.matmul(ps[6 + c], tT[:, k, :], wpg[:, k, c * HALF:(c + 1) * HALF],
                                    start=(k == 0), stop=(k == KC - 1))
                last.then_inc(tail_gate_made, 1)

            def tail_embed(t):
                if t < TILES - 1:
                    pe.wait_ge(tail_gate_ready, 2 * t + 2)
                else:
                    pe.wait_ge(sum_out, t)
                for c in range(2):
                    for k in range(2):
                        last = T.matmul(ps[EMBED[t] + c], pT[:, k, t * P:(t + 1) * P], wple[:, k, c * HALF:(c + 1) * HALF],
                                        start=(k == 0), stop=(k == 1))
                last.then_inc(tail_embed_made, 1)

            pe.wait_ge(wo_added, 2 * TILES)
            for t in range(TILES):
                if t == 1:
                    pe.wait_ge(keyscores_out, 4 * TILES)
                if t == 0:
                    open_sum(0).then_inc(column_used, GRP + 1)
                else:
                    open_sum(t)
                for seg in range(SEGS[t]):
                    first, pairs = segment(t, seg)
                    with pe.Fori(0, pairs) as i:
                        for s in range(SLOTS):
                            pe.wait_ge(diag_ready, i * SLOTS + (first * GRP + s + 1))
                            for c in range(2):
                                last = T.matmul(ps[2 + 2 * (t % 2) + c], diag[:, s, :],
                                                rows[:, s, D + c * HALF:D + (c + 1) * HALF], start=False, stop=False)
                            last.then_inc(column_used, 1)
                    if t == 0:
                        if seg == 0:
                            turn_others()
                        if seg == 1:
                            pe.wait_ge(hT_ready, 2 * KC + 2)
                        if 1 <= seg <= 8:
                            other_queries(2 * seg - 2)
                            other_queries(2 * seg - 1)
                        if seg in SCORE_SEGS:
                            later = SCORE_SEGS.index(seg) + 1
                            if later == 1:
                                pe.wait_ge(query_out, 4 + 2 * PH)
                            pe.wait_ge(keyscores_out, 4 * later)
                            for c in range(4):
                                scores(later, c)
                    if t:
                        if seg == 1:
                            tail_turn(t - 1)
                        if seg in (3, 4):
                            tail_gate(t - 1, seg - 3)
                        if seg == 5:
                            tail_embed(t - 1)
                        if seg == 6 and t == TILES - 1:
                            tail_embed(t)
                for c in range(2):
                    last = T.matmul(ps[2 + 2 * (t % 2) + c], zero[:, :], xs[:, t, c * HALF:(c + 1) * HALF],
                                    start=False, stop=True)
                last.then_inc(sum_ready, 1)
            tail_turn(TILES - 1)
            for c in range(2):
                tail_gate(TILES - 1, c)


OUT_SHAPE = (1, S, D)


def lay_out(i):
    f = {k: np.asarray(v) for k, v in i.items()}
    w_in = f["w_in"][0]
    ar = np.arange

    def by_chunk(w, cols):
        return w[:, cols].reshape(KC, P, len(cols)).transpose(1, 0, 2).reshape(P, -1)

    q_a, k_a, v_a, q_b = 0, 512, 640, 768
    k_c, v_c, k_s, v_s, k_w, v_w, b_g, m_g = 1280, 1408, 1536, 1664, 1792, 1920, 2048, 2072
    pair = lambda base, r: np.concatenate([ar(DH) + base + r * DH, ar(DH) + base + (r + REP) * DH])
    run = lambda base: ar(P) + base
    zcols = [pair(q_a, r) for r in range(REP)] + [run(k_a)] + [pair(q_b, r) for r in range(REP)]
    zcols += [run(k_s), run(k_w), run(k_c), run(v_c)]
    blocks = [by_chunk(w_in, c) for c in zcols]
    nat = np.concatenate([run(v_a), run(v_s), run(v_w), ar(3 * HEADS) + b_g])
    wn = np.zeros((P, KC, HALF), np.float32)
    wn[:, :, :NAT_COLS] = by_chunk(w_in, nat).reshape(P, KC, NAT_COLS)
    for w in ("cmp_k_w1", "cmp_v_w1"):
        w1 = f[w][0].reshape(LPAIR, P, CMP_HID)
        blocks += [w1[4 * b:4 * b + 4].transpose(1, 0, 2).reshape(P, D) for b in range(4)]
    blocks += [wn[:, 2 * b:2 * b + 2].reshape(P, D) for b in range(NATB)]
    for m in range(KC):
        blocks += [by_chunk(w_in, run(m_g + m * P)), by_chunk(w_in, run(m_g + D + m * P))]
        up = np.concatenate([f["w_up_a"][0], f["w_up_b"][0]])
        blocks.append(by_chunk(up, run(m * P)))
    blocks += [f["w_o"][0][k * P:(k + 1) * P] for k in range(KC)]
    blocks += [by_chunk(f["peer_wq"][0], run(j * P)) for j in range(2 * PH)]
    pos = f["cmp_pos"][0].T
    w2 = np.stack([f["cmp_k_w2"][0].reshape(2, P, DH), f["cmp_v_w2"][0].reshape(2, P, DH)])
    small = np.concatenate([
        f["g_mix"][0].reshape(KC, P).T, f["g_ple"][0].reshape(KC, P).T, np.concatenate([pos, pos]),
        np.broadcast_to(f["a_sink"][0].reshape(1, HEADS), (P, HEADS)),
        w2.transpose(2, 0, 1, 3).reshape(P, -1),
        f["peer_k1"][0].T, f["peer_k2"][0].T], axis=1)
    rel = f["rel_bias"]
    return {
        "x": f["x"][0],
        "small": small,
        "rel_bias": rel,
        "hot": bucket_onehot(),
        "wpack": np.stack(blocks),
        "g_ffn": np.broadcast_to(f["g_ffn"][0][None], (P, D)),
        "g_final": np.broadcast_to(f["g_final"][None], (P, D)),
        "pT": f["p"][0, 0].T.reshape(2, P, S).transpose(1, 0, 2),
        "w_ple": f["w_ple"][0].reshape(2, P, D).transpose(1, 0, 2),
        "w_pg": f["w_ple_gate"][0].reshape(KC, P, D).transpose(1, 0, 2),
        "uv": np.concatenate([f["peer_u"][0], f["peer_v"][0]], axis=1),
    }


def kernel(**inputs):
    import concourse.bacc as bacc
    from concourse.bass_utils import run_bass_kernel_spmd

    nc = bacc.Bacc("TRN2", target_bir_lowering=False, num_devices=1)
    arrays, aps = {}, {}
    for name, v in lay_out(inputs).items():
        v = np.ascontiguousarray(v)
        arrays[f"in_{name}"] = v
        aps[name] = nc.dram_tensor(f"in_{name}", v.shape, mybir.dt.from_np(v.dtype), kind="ExternalInput").ap()
    out = nc.dram_tensor("out", (S, D), mybir.dt.float32, kind="ExternalOutput").ap()
    build(nc, aps, out)
    got = run_bass_kernel_spmd(nc, [arrays], core_ids=[0])
    return got.results[0]["out"].reshape(OUT_SHAPE)
```
